# Optimizing a Trainium2 kernel written in Bass

```python
import jax, jax.numpy as jnp
from jax import lax
import numpy as np
import math
import jax
import jax.numpy as jnp

D_MODEL = 1024
BATCH = 1
SEQ = 256
DEPTH = 4

N_MIXERS = 3
EXPAND = 2
D_INNER = EXPAND * D_MODEL
CONF_KERNEL = 31
SHORT_KERNEL = 3
FOX_HEADS = 16
FOX_HEAD_DIM = D_INNER // FOX_HEADS
Q_BLOCK = 128
NORM_EPS = 1e-6
N_A = (DEPTH + 2) // 3
N_B = (DEPTH + 1) // 3
N_C = DEPTH // 3


def rms_norm(x, g):
    xf = x.astype(jnp.float32)
    y = xf * lax.rsqrt(jnp.mean(xf * xf, axis=-1, keepdims=True) + NORM_EPS)
    return (y * g.astype(jnp.float32)).astype(x.dtype)

def layer_norm(x, g, b):
    xf = x.astype(jnp.float32)
    mu = jnp.mean(xf, axis=-1, keepdims=True)
    var = jnp.mean(jnp.square(xf - mu), axis=-1, keepdims=True)
    y = (xf - mu) * lax.rsqrt(var + NORM_EPS)
    return (y * g.astype(jnp.float32) + b.astype(jnp.float32)).astype(x.dtype)

def causal_depthwise_conv(x, w):
    k_width, channels = w.shape
    kern = w[:, None, :].astype(x.dtype)
    return lax.conv_general_dilated(
        x, kern, window_strides=(1,), padding=[(k_width - 1, 0)],
        dimension_numbers=("NWC", "WIO", "NWC"), feature_group_count=channels)

def conformer_conv_mixer(h, w_in, conv_w, conv_b, ln_g, ln_b, w_out):
    proj = h @ w_in
    val, glu_gate, z = jnp.split(proj, 3, axis=-1)
    u = val * jax.nn.sigmoid(glu_gate)
    u = causal_depthwise_conv(u, conv_w) + conv_b
    u = jax.nn.silu(layer_norm(u, ln_g, ln_b))
    return (u * jax.nn.silu(z)) @ w_out

def blocked_forgetting_attention(q, k, v, c):
    b, s_len, n_h, d_h = q.shape
    n_blocks = s_len // Q_BLOCK
    scale = d_h ** -0.5
    k_pos = jnp.arange(s_len)

    def one_block(i):
        start = i * Q_BLOCK
        q_blk = lax.dynamic_slice_in_dim(q, start, Q_BLOCK, axis=1)
        c_blk = lax.dynamic_slice_in_dim(c, start, Q_BLOCK, axis=2)
        logits = jnp.einsum("bqhd,bkhd->bhqk", q_blk, k,
                            preferred_element_type=jnp.float32) * scale
        logits = logits + c_blk[..., :, None] - c[..., None, :]
        q_pos = start + jnp.arange(Q_BLOCK)
        causal = k_pos[None, :] <= q_pos[:, None]
        logits = jnp.where(causal, logits, -jnp.inf)
        p = jax.nn.softmax(logits, axis=-1)
        return jnp.einsum("bhqk,bkhd->bqhd", p.astype(v.dtype), v)

    out = lax.map(one_block, jnp.arange(n_blocks))
    return out.transpose(1, 0, 2, 3, 4).reshape(b, s_len, n_h, d_h)

def forgetting_attention_mixer(h, w_in, f_bias, q_norm_g, k_norm_g, w_out):
    b, s_len, _ = h.shape
    proj = h @ w_in
    q, k, v, z, f_logit = jnp.split(
        proj, [D_INNER, 2 * D_INNER, 3 * D_INNER, 4 * D_INNER], axis=-1)
    q = rms_norm(q.reshape(b, s_len, FOX_HEADS, FOX_HEAD_DIM), q_norm_g)
    k = rms_norm(k.reshape(b, s_len, FOX_HEADS, FOX_HEAD_DIM), k_norm_g)
    v = v.reshape(b, s_len, FOX_HEADS, FOX_HEAD_DIM)
    log_f = jax.nn.log_sigmoid((f_logit + f_bias).astype(jnp.float32))
    c = jnp.cumsum(log_f, axis=1).transpose(0, 2, 1)
    o = blocked_forgetting_attention(q, k, v, c).reshape(b, s_len, D_INNER)
    return (o * jax.nn.silu(z)) @ w_out

def short_conv_mixer(h, w_in, conv_w, w_out):
    proj = h @ w_in
    u, b_gate, c_gate, z = jnp.split(proj, 4, axis=-1)
    y = b_gate * causal_depthwise_conv(c_gate * u, conv_w)
    return (y * jax.nn.silu(z)) @ w_out

def first_inputs(seed: int = 0) -> dict:
    key = jax.random.key(seed)
    ks = jax.random.split(key, 20)
    f32 = jnp.float32
    nrm = lambda k, shape, s: jax.random.normal(k, shape, f32) * s
    d, e, h = D_MODEL, D_INNER, FOX_HEADS
    return {
        "x": jax.random.normal(ks[0], (BATCH, SEQ, d), f32),
        "a_norm": 1.0 + nrm(ks[1], (N_A, d), 0.05),
        "a_w_in": nrm(ks[2], (N_A, d, 3 * e), d ** -0.5),
        "a_conv_w": nrm(ks[3], (N_A, CONF_KERNEL, e), CONF_KERNEL ** -0.5),
        "a_conv_b": nrm(ks[4], (N_A, e), 0.01),
        "a_ln_g": 1.0 + nrm(ks[5], (N_A, e), 0.05),
        "a_ln_b": nrm(ks[6], (N_A, e), 0.01),
        "a_w_out": nrm(ks[7], (N_A, e, d), e ** -0.5),
        "b_norm": 1.0 + nrm(ks[8], (N_B, d), 0.05),
        "b_w_in": nrm(ks[9], (N_B, d, 4 * e + h), d ** -0.5),
        "b_f_bias": 2.0 + nrm(ks[10], (N_B, h), 0.5),
        "b_q_norm": 1.0 + nrm(ks[11], (N_B, FOX_HEAD_DIM), 0.05),
        "b_k_norm": 1.0 + nrm(ks[12], (N_B, FOX_HEAD_DIM), 0.05),
        "b_w_out": nrm(ks[13], (N_B, e, d), e ** -0.5),
        "c_norm": 1.0 + nrm(ks[14], (N_C, d), 0.05),
        "c_w_in": nrm(ks[15], (N_C, d, 4 * e), d ** -0.5),
        "c_conv_w": nrm(ks[16], (N_C, SHORT_KERNEL, e), SHORT_KERNEL ** -0.5),
        "c_w_out": nrm(ks[17], (N_C, e, d), e ** -0.5),
    }

def first_block(x, a_norm, a_w_in, a_conv_w, a_conv_b, a_ln_g, a_ln_b, a_w_out,
              b_norm, b_w_in, b_f_bias, b_q_norm, b_k_norm, b_w_out,
              c_norm, c_w_in, c_conv_w, c_w_out):
    for i in range(DEPTH):
        kind, j = i % N_MIXERS, i // N_MIXERS
        if kind == 0:
            hn = rms_norm(x, a_norm[j])
            x = x + conformer_conv_mixer(hn, a_w_in[j], a_conv_w[j], a_conv_b[j],
                                         a_ln_g[j], a_ln_b[j], a_w_out[j])
        elif kind == 1:
            hn = rms_norm(x, b_norm[j])
            x = x + forgetting_attention_mixer(hn, b_w_in[j], b_f_bias[j], b_q_norm[j],
                                               b_k_norm[j], b_w_out[j])
        else:
            hn = rms_norm(x, c_norm[j])
            x = x + short_conv_mixer(hn, c_w_in[j], c_conv_w[j], c_w_out[j])
    return x


DEPTH_2 = 1

HEAD_DIM = 64

REL_BUCKETS = 32
REL_MAX_DIST = 2048

A_HEADS = 8
A_IDX_HEADS = 4
A_IDX_DIM = 64
A_TOPK_MAX = 256

B_HEADS = 8
B_KV_HEADS = 2
B_GROUP = B_HEADS // B_KV_HEADS
B_CMP_LEN = 32
B_CMP_STRIDE = 16
B_SEL_LEN = 64
B_SEL_TOPK_MAX = 16
B_WINDOW = 512
B_Q_BLOCK = 64

C_GROUPS = ((128, 1), (512, 4), (2048, 16))
C_HEADS_PER_GROUP = 4
C_HEADS = C_HEADS_PER_GROUP * len(C_GROUPS)
C_PAD = 2048

REL_HEADS = A_HEADS + B_HEADS + C_HEADS

D_FF = ((8 * D_MODEL + 3 * 256 - 1) // (3 * 256)) * 256

IN_SIZES = (
    A_HEADS * HEAD_DIM,
    HEAD_DIM,
    HEAD_DIM,
    A_IDX_HEADS * A_IDX_DIM,
    A_IDX_DIM,
    A_IDX_HEADS,
    B_HEADS * HEAD_DIM,
    6 * B_KV_HEADS * HEAD_DIM,
    3 * B_HEADS,
    3 * C_HEADS * HEAD_DIM,
    3 * D_MODEL,
)
IN_TOTAL = sum(IN_SIZES)


def _rms(x, g):
    xf = x.astype(jnp.float32)
    y = xf * lax.rsqrt(jnp.mean(xf * xf, axis=-1, keepdims=True) + NORM_EPS)
    return (y * g.astype(jnp.float32)).astype(x.dtype)

def _split_last(y, sizes):
    out, off = [], 0
    for n in sizes:
        out.append(y[..., off:off + n])
        off += n
    return out

def _rel_bucket(dist):
    n = jnp.maximum(dist, 0)
    exact = REL_BUCKETS // 2
    nf = jnp.maximum(n, 1).astype(jnp.float32)
    large = exact + (jnp.log(nf / exact) / math.log(REL_MAX_DIST / exact)
                     * (REL_BUCKETS - exact)).astype(jnp.int32)
    return jnp.where(n < exact, n, jnp.minimum(large, REL_BUCKETS - 1))

def _masked_softmax(logits, mask):
    s = jnp.where(mask, logits, -jnp.inf)
    m = jnp.max(s, axis=-1, keepdims=True)
    m = jnp.where(jnp.isfinite(m), m, 0.0)
    e = jnp.exp(s - m)
    den = jnp.sum(e, axis=-1, keepdims=True)
    p = e / jnp.maximum(den, 1e-30)
    lse = (m + jnp.log(den))[..., 0]
    return p, lse

def _sweep(fn, seq, block):
    out = lax.map(fn, jnp.arange(seq // block))
    out = jnp.moveaxis(out, 0, 1)
    return out.reshape((out.shape[0], seq) + out.shape[3:])

_gather_rows = jax.vmap(lambda a, i: a[i])

def _dsa_attention(q, k, v, iq, ik, iw, rel_tab):
    seq = q.shape[1]
    topk = min(A_TOPK_MAX, seq // 4)
    scale = HEAD_DIM ** -0.5
    keys = jnp.arange(seq)

    def block(i):
        q0 = i * Q_BLOCK
        t = q0 + jnp.arange(Q_BLOCK)
        qb = lax.dynamic_slice_in_dim(q, q0, Q_BLOCK, axis=1)
        iqb = lax.dynamic_slice_in_dim(iq, q0, Q_BLOCK, axis=1)
        iwb = lax.dynamic_slice_in_dim(iw, q0, Q_BLOCK, axis=1).astype(jnp.float32)
        rel = jax.nn.relu(jnp.einsum("bqhd,bsd->bqhs", iqb, ik, preferred_element_type=jnp.float32))
        score = jnp.einsum("bqhs,bqh->bqs", rel, iwb)
        score = jnp.where(keys[None, None, :] <= t[None, :, None], score, -jnp.inf)
        _, idx = lax.top_k(score, topk)
        kg = _gather_rows(k, idx)
        vg = _gather_rows(v, idx)
        dist = t[None, :, None] - idx
        bias = jnp.moveaxis(rel_tab[_rel_bucket(dist)], -1, 1)
        logits = jnp.einsum("bqhd,bqkd->bhqk", qb, kg, preferred_element_type=jnp.float32) * scale + bias
        p, _ = _masked_softmax(logits, (dist >= 0)[:, None])
        return jnp.einsum("bhqk,bqkd->bqhd", p.astype(vg.dtype), vg).astype(q.dtype)

    o = _sweep(block, seq, Q_BLOCK)
    return o.reshape(o.shape[:2] + (A_HEADS * HEAD_DIM,))

def _nsa_attention(q, kc, vc, ks, vs, kw, vw, gates, cmp_pos, cmp_w, k_gain, rel_tab):
    bsz, seq = q.shape[:2]
    G, Hg, Dh = B_KV_HEADS, B_GROUP, HEAD_DIM
    scale = Dh ** -0.5
    n_cmp = (seq - B_CMP_LEN) // B_CMP_STRIDE + 1
    n_sel = seq // B_SEL_LEN
    n_top = min(B_SEL_TOPK_MAX, n_sel)

    cidx = jnp.arange(n_cmp)[:, None] * B_CMP_STRIDE + jnp.arange(B_CMP_LEN)[None, :]

    def compress(src, pos, w):
        blk = src[:, cidx] + pos[:, None, :]
        return jnp.einsum("bnlgd,lde->bnge", blk, w)

    kcmp = _rms(compress(kc, cmp_pos[0], cmp_w[0]), k_gain)
    vcmp = compress(vc, cmp_pos[1], cmp_w[1])
    cstart = cidx[:, 0]
    cend = cidx[:, -1]
    sstart = jnp.arange(n_sel) * B_SEL_LEN
    overlap = ((cstart[:, None] < sstart[None, :] + B_SEL_LEN)
               & (cstart[:, None] + B_CMP_LEN > sstart[None, :])).astype(jnp.float32)
    ksb = jnp.moveaxis(ks.reshape(bsz, n_sel, B_SEL_LEN, G, Dh), 3, 1)
    vsb = jnp.moveaxis(vs.reshape(bsz, n_sel, B_SEL_LEN, G, Dh), 3, 1)
    wpad = ((0, 0), (B_WINDOW, 0), (0, 0), (0, 0))
    kw_pad = jnp.pad(kw, wpad)
    vw_pad = jnp.pad(vw, wpad)
    tab = rel_tab.reshape(REL_BUCKETS, G, Hg)
    sel_blocks = jnp.arange(n_sel)
    gather_blocks = jax.vmap(jax.vmap(lambda a, i: a[i]))
    bias_per_group = jax.vmap(lambda tb, bk: tb[bk], in_axes=(1, 1), out_axes=1)

    def block(i):
        q0 = i * B_Q_BLOCK
        t = q0 + jnp.arange(B_Q_BLOCK)
        qb = lax.dynamic_slice_in_dim(q, q0, B_Q_BLOCK, axis=1).reshape(bsz, B_Q_BLOCK, G, Hg, Dh)
        gb = lax.dynamic_slice_in_dim(gates, q0, B_Q_BLOCK, axis=1).reshape(bsz, B_Q_BLOCK, G, Hg, 3)
        lc = jnp.einsum("bqghd,bngd->bghqn", qb, kcmp, preferred_element_type=jnp.float32) * scale
        pc, _ = _masked_softmax(lc, cend[None, :] <= t[:, None])
        oc = jnp.einsum("bghqn,bngd->bqghd", pc.astype(vcmp.dtype), vcmp)
        imp = jnp.einsum("bghqn,nm->bgqm", pc, overlap)
        jt = (t // B_SEL_LEN)[:, None]
        forced = (sel_blocks[None] == 0) | (sel_blocks[None] == jt) | (sel_blocks[None] == jt - 1)
        imp = jnp.where(forced, jnp.inf, jnp.where(sel_blocks[None] <= jt, imp, -jnp.inf))
        _, sel = lax.top_k(imp, n_top)
        kg = gather_blocks(ksb, sel).reshape(bsz, G, B_Q_BLOCK, n_top * B_SEL_LEN, Dh)
        vg = gather_blocks(vsb, sel).reshape(bsz, G, B_Q_BLOCK, n_top * B_SEL_LEN, Dh)
        pos = (sel[..., None] * B_SEL_LEN + jnp.arange(B_SEL_LEN)).reshape(bsz, G, B_Q_BLOCK, -1)
        dist = t[None, None, :, None] - pos
        bias_s = jnp.moveaxis(bias_per_group(tab, _rel_bucket(dist)), -1, 2)
        ls = jnp.einsum("bqghd,bgqkd->bghqk", qb, kg, preferred_element_type=jnp.float32) * scale + bias_s
        ps, _ = _masked_softmax(ls, (dist >= 0)[:, :, None])
        osel = jnp.einsum("bghqk,bgqkd->bqghd", ps.astype(vg.dtype), vg)
        kwb = lax.dynamic_slice_in_dim(kw_pad, q0, B_Q_BLOCK + B_WINDOW, axis=1)
        vwb = lax.dynamic_slice_in_dim(vw_pad, q0, B_Q_BLOCK + B_WINDOW, axis=1)
        kpos = q0 - B_WINDOW + jnp.arange(B_Q_BLOCK + B_WINDOW)
        dw = t[:, None] - kpos[None, :]
        mw = (dw >= 0) & (dw < B_WINDOW) & (kpos[None, :] >= 0)
        bias_w = jnp.transpose(tab[_rel_bucket(dw)], (2, 3, 0, 1))
        lw = jnp.einsum("bqghd,bkgd->bghqk", qb, kwb, preferred_element_type=jnp.float32) * scale + bias_w
        pw, _ = _masked_softmax(lw, mw)
        ow = jnp.einsum("bghqk,bkgd->bqghd", pw.astype(vwb.dtype), vwb)
        o = gb[..., 0:1] * oc + gb[..., 1:2] * osel + gb[..., 2:3] * ow
        return o.reshape(bsz, B_Q_BLOCK, G * Hg * Dh).astype(q.dtype)

    return _sweep(block, seq, B_Q_BLOCK)

def _dilated_attention(q, k, v, rel_tab):
    bsz, seq = q.shape[:2]
    scale = HEAD_DIM ** -0.5
    pad = ((0, 0), (C_PAD, 0), (0, 0), (0, 0))
    hsl = [slice(g * C_HEADS_PER_GROUP, (g + 1) * C_HEADS_PER_GROUP) for g in range(len(C_GROUPS))]
    kps = [jnp.pad(k[:, :, hs], pad) for hs in hsl]
    vps = [jnp.pad(v[:, :, hs], pad) for hs in hsl]

    def block(i):
        q0 = i * Q_BLOCK
        t = q0 + jnp.arange(Q_BLOCK)
        qb = lax.dynamic_slice_in_dim(q, q0, Q_BLOCK, axis=1)
        outs, lses = [], []
        for gi, (win, dil) in enumerate(C_GROUPS):
            steps = jnp.arange(win // dil + 1) * dil
            pos = t[:, None] - steps[None, :]
            kg = jnp.take(kps[gi], pos + C_PAD, axis=1)
            vg = jnp.take(vps[gi], pos + C_PAD, axis=1)
            bias = rel_tab[_rel_bucket(steps), hsl[gi]].T[None, :, None, :]
            logits = jnp.einsum("bqhd,bqkhd->bhqk", qb[:, :, hsl[gi]], kg,
                                preferred_element_type=jnp.float32) * scale + bias
            p, lse = _masked_softmax(logits, (pos >= 0)[None, None])
            outs.append(jnp.einsum("bhqk,bqkhd->bqhd", p.astype(vg.dtype), vg))
            lses.append(lse)
        w = jax.nn.softmax(jnp.stack(lses), axis=0)
        w = jnp.transpose(w, (0, 1, 3, 2))[..., None]
        o = w[0] * outs[0]
        for gi in range(1, len(C_GROUPS)):
            o = o + w[gi] * outs[gi]
        return o.reshape(bsz, Q_BLOCK, C_HEADS_PER_GROUP * HEAD_DIM).astype(q.dtype)

    return _sweep(block, seq, Q_BLOCK)

def second_inputs(seed: int = 0) -> dict:
    key = jax.random.key(seed)
    ks = jax.random.split(key, 14)

    def nrm(k, shape, scale):
        return jax.random.normal(k, shape, jnp.float32) * scale

    return {
        "x": nrm(ks[0], (BATCH, SEQ, D_MODEL), 1.0),
        "norm1_g": 1.0 + nrm(ks[1], (DEPTH_2, D_MODEL), 0.1),
        "norm2_g": 1.0 + nrm(ks[2], (DEPTH_2, D_MODEL), 0.1),
        "w_in": nrm(ks[3], (DEPTH_2, D_MODEL, IN_TOTAL), D_MODEL ** -0.5),
        "qk_norm_g": 1.0 + nrm(ks[4], (DEPTH_2, 6, HEAD_DIM), 0.1),
        "nsa_cmp_pos": nrm(ks[5], (DEPTH_2, 2, B_CMP_LEN, HEAD_DIM), 0.5),
        "nsa_cmp_w": nrm(ks[6], (DEPTH_2, 2, B_CMP_LEN, HEAD_DIM, HEAD_DIM), (B_CMP_LEN * HEAD_DIM) ** -0.5),
        "w_branch_a": nrm(ks[7], (DEPTH_2, A_HEADS * HEAD_DIM, D_MODEL), (A_HEADS * HEAD_DIM) ** -0.5),
        "w_branch_b": nrm(ks[8], (DEPTH_2, B_HEADS * HEAD_DIM, D_MODEL), (B_HEADS * HEAD_DIM) ** -0.5),
        "w_branch_c": nrm(ks[9], (DEPTH_2, C_HEADS_PER_GROUP * HEAD_DIM, D_MODEL), (C_HEADS_PER_GROUP * HEAD_DIM) ** -0.5),
        "w_out": nrm(ks[10], (DEPTH_2, D_MODEL, D_MODEL), D_MODEL ** -0.5),
        "w_ffn_in": nrm(ks[11], (DEPTH_2, D_MODEL, 2 * D_FF), D_MODEL ** -0.5),
        "w_ffn_out": nrm(ks[12], (DEPTH_2, D_FF, D_MODEL), D_FF ** -0.5),
        "rel_bias": nrm(ks[13], (REL_BUCKETS, REL_HEADS), 0.5),
    }

def second_block(x, norm1_g, norm2_g, w_in, qk_norm_g, nsa_cmp_pos, nsa_cmp_w, w_branch_a, w_branch_b,
              w_branch_c, w_out, w_ffn_in, w_ffn_out, rel_bias):
    bsz, seq, _ = x.shape
    rel_a = rel_bias[:, :A_HEADS]
    rel_b = rel_bias[:, A_HEADS:A_HEADS + B_HEADS]
    rel_c = rel_bias[:, A_HEADS + B_HEADS:]
    for layer in range(DEPTH_2):
        h = _rms(x, norm1_g[layer])
        (a_q, a_k, a_v, i_q, i_k, i_w, b_q, b_kv, b_g, c_qkv, mix_g) = _split_last(h @ w_in[layer], IN_SIZES)
        qk = qk_norm_g[layer]
        a_q = _rms(a_q.reshape(bsz, seq, A_HEADS, HEAD_DIM), qk[0])
        a_k = _rms(a_k, qk[1])
        y_a = _dsa_attention(a_q, a_k, a_v, i_q.reshape(bsz, seq, A_IDX_HEADS, A_IDX_DIM), i_k, i_w,
                             rel_a) @ w_branch_a[layer]
        b_q = _rms(b_q.reshape(bsz, seq, B_HEADS, HEAD_DIM), qk[2])
        b_kv = b_kv.reshape(bsz, seq, 6, B_KV_HEADS, HEAD_DIM)
        b_gates = jax.nn.sigmoid(b_g).reshape(bsz, seq, B_HEADS, 3)
        y_b = _nsa_attention(b_q, b_kv[:, :, 0], b_kv[:, :, 1], _rms(b_kv[:, :, 2], qk[3]), b_kv[:, :, 3],
                             _rms(b_kv[:, :, 4], qk[3]), b_kv[:, :, 5], b_gates, nsa_cmp_pos[layer],
                             nsa_cmp_w[layer], qk[3], rel_b) @ w_branch_b[layer]
        c_qkv = c_qkv.reshape(bsz, seq, 3, C_HEADS, HEAD_DIM)
        y_c = _dilated_attention(_rms(c_qkv[:, :, 0], qk[4]), _rms(c_qkv[:, :, 1], qk[5]), c_qkv[:, :, 2],
                                 rel_c) @ w_branch_c[layer]
        g = jax.nn.sigmoid(mix_g).reshape(bsz, seq, 3, D_MODEL)
        x = x + (g[:, :, 0] * y_a + g[:, :, 1] * y_b + g[:, :, 2] * y_c) @ w_out[layer]
        h = _rms(x, norm2_g[layer])
        gate, up = jnp.split(h @ w_ffn_in[layer], 2, axis=-1)
        x = x + (jax.nn.silu(gate) * up) @ w_ffn_out[layer]
    return x


def setup_inputs(seed=0):
    out = dict(first_inputs(seed))
    for name, value in second_inputs(seed + 1).items():
        if name != "x":
            out[name + "_2"] = value
    return out


def reference(
    x, a_norm, a_w_in, a_conv_w, a_conv_b, a_ln_g, a_ln_b, a_w_out, b_norm, b_w_in, b_f_bias,
    b_q_norm, b_k_norm, b_w_out, c_norm, c_w_in, c_conv_w, c_w_out, norm1_g_2, norm2_g_2,
    w_in_2, qk_norm_g_2, nsa_cmp_pos_2, nsa_cmp_w_2, w_branch_a_2, w_branch_b_2, w_branch_c_2,
    w_out_2, w_ffn_in_2, w_ffn_out_2, rel_bias_2,
):
    x = first_block(
        x, a_norm, a_w_in, a_conv_w, a_conv_b, a_ln_g, a_ln_b, a_w_out, b_norm, b_w_in,
        b_f_bias, b_q_norm, b_k_norm, b_w_out, c_norm, c_w_in, c_conv_w, c_w_out,
    )
    return second_block(
        x, norm1_g_2, norm2_g_2, w_in_2, qk_norm_g_2, nsa_cmp_pos_2, nsa_cmp_w_2, w_branch_a_2,
        w_branch_b_2, w_branch_c_2, w_out_2, w_ffn_in_2, w_ffn_out_2, rel_bias_2,
    )


_drawn_inputs = setup_inputs


def setup_inputs(seed=0):
    import zlib

    import numpy as np

    out = dict(_drawn_inputs(seed))
    spreads = {}
    factors = {'a_conv_b': 3.17,
     'a_ln_b': 5.69,
     'b_q_norm': 3.242,
     'b_k_norm': 3.532,
     'qk_norm_g_2': 2.785}
    for name, (base, spread) in spreads.items():
        noise = np.random.default_rng([zlib.crc32(name.encode()), seed]).standard_normal(out[name].shape)
        drawn = base * np.exp(spread * noise) if base else spread * noise
        out[name] = jnp.asarray(drawn.astype(out[name].dtype))
    for name, factor in factors.items():
        out[name] = (out[name] * factor).astype(out[name].dtype)
    return out
```

```python
from contextlib import ExitStack

import numpy as np

import concourse.bass as bass
from concourse import mybir

F32 = mybir.dt.float32
ALU = mybir.AluOpType
ACT = mybir.ActivationFunctionType
AX = mybir.AxisListType.X

P = 128
S = 256
TB = S // P
D = 1024
KD = D // P
E = 2048
KE = E // P
NEG = -1e30
EPS = 1e-6
TAPS = 31
TAPS_DVE = 19
TAPS_POOL = TAPS - TAPS_DVE
SHORT = 3
FH = 16
FD = E // FH
HD = 64
TOPK = 64
A_H, IDX_H, B_H, B_G, C_H, C_SLOTS, C_GROUPS = 8, 4, 8, 2, 12, 4, ((128, 1), (512, 4), (2048, 16))
NCMP = (S - 32) // 16 + 1
LC = 16
FF = 2816
KF = FF // P
OFF_AK, OFF_AV, OFF_IQ, OFF_IK, OFF_IW, OFF_BQ = 512, 576, 640, 896, 960, 964
OFF_KV, OFF_BG, OFF_CQ, OFF_CK, OFF_CV, OFF_MIX = 1476, 2244, 2268, 3036, 3804, 4572
RING = 4
UNIT = KD * 2 * P
TABLE = 384
HEADS2 = A_H + B_H + C_H

C_ID, C_ONE, C_B64, C_E1, C_E2 = 0, 128, 256, 384, 384 + 31
C_MASK = C_E2 + 62
C_CMP = C_MASK + S
C_SEL = C_CMP + 2 * NCMP
NORMED = 13
C_END = C_SEL + NORMED * P


def rel_bucket(dist):
    n = np.maximum(dist, 0)
    nf = np.maximum(n, 1).astype(np.float32)
    large = 16 + (np.log(nf / np.float32(16)) / np.float32(np.log(2048 / 16)) * np.float32(16)).astype(np.int32)
    return np.where(n < 16, n, np.minimum(large, 31))


def constants():
    c = np.zeros((P, C_END), np.float32)
    p = np.arange(P)
    c[:, C_ID:C_ID + P] = np.eye(P)
    c[:, C_ONE:C_ONE + P] = 1.0
    c[:, C_B64:C_B64 + P] = (p[:, None] // 64) == (p[None, :] // 64)
    c[:, C_E1 + 15] = 1.0
    c[:64, C_E2 + 30] = 1.0
    c[64:, C_E2 + 31] = 1.0
    c[:, C_MASK:C_MASK + S] = np.where(P + p[:, None] - np.arange(S)[None, :] >= 0, 0.0, NEG)
    for tb in range(TB):
        end = 16 * np.arange(NCMP)[None, :] + 31
        c[:, C_CMP + tb * NCMP:C_CMP + (tb + 1) * NCMP] = np.where(end <= tb * P + p[:, None], 0.0, NEG)
    for g in range(NORMED):
        for half in range(2):
            c[2 * g + half, C_SEL + g * P + 64 * half:C_SEL + g * P + 64 * half + 64] = 1.0
    hot = np.zeros((33, 4, TABLE), np.float32)
    dist = S - 1 - np.arange(TABLE)
    for v in range(4):
        ok = dist >= 0
        if v:
            window, step = C_GROUPS[v - 1]
            ok &= (dist <= window) & (dist % step == 0)
        hot[rel_bucket(dist)[ok], v, np.nonzero(ok)[0]] = 1.0
        hot[32, v, ~ok] = NEG
    return c, hot.reshape(33, 4 * TABLE)


def program(nc, t, out):
    ctx = ExitStack()
    with ctx:
        def sb(name, cols, rows=P):
            return ctx.enter_context(nc.sbuf_tensor(name, [rows, cols], F32))

        def sem(name):
            return ctx.enter_context(nc.semaphore(name))

        cst = sb("cst", C_END)
        ident = cst[:, C_ID:C_ID + P]
        ones = cst[:, C_ONE:C_ONE + P]
        blk64 = cst[:, C_B64:C_B64 + P]
        xT = sb("xT", KD * S)[:, :].rearrange("p (k t) -> p k t", t=S)
        xn = sb("xn", KD * S)[:, :].rearrange("p (k t) -> p k t", t=S)
        sqb = sb("sqb", KD * S)[:, :].rearrange("p (k t) -> p k t", t=S)
        std = sb("std", 2 * S)
        rr = sb("rr", 2 * S)
        ring = sb("ring", RING * UNIT)
        wide = sb("wide", 38 * S)
        yb = wide[:, 0:KE * S].rearrange("p (k t) -> p k t", t=S)
        zb = wide[:, KE * S:38 * S].rearrange("p (k t) -> p k t", t=S)
        T = wide[:, 0:HEADS2 * S].rearrange("p (h s) -> p h s", s=S)
        oT = wide[:, HEADS2 * S:38 * S].rearrange("p (k t) -> p k t", t=S)
        qk = sb("qk", 16 * 2 * S)[:, :].rearrange("p (g a t) -> p g a t", a=2, t=S)
        vb_flat = sb("vb", TB * E)
        vb = vb_flat[:, :].rearrange("p (b n) -> p b n", b=TB)
        mix = sb("mix", 24 * S)[:, :].rearrange("p (k t) -> p k t", t=S)
        cols = sb("cols", 88 + 96 + 48)
        convw = sb("convw", 2 * TAPS * KE)
        taps = convw[:, :].rearrange("p (j k c) -> p j k c", j=2, k=TAPS)
        small = sb("small", 256)
        scratch = sb("scratch", 4608)
        hot = scratch[0:33, 0:4 * TABLE]
        tabs = scratch[0:16, 4 * TABLE:8 * TABLE].rearrange("p (v j) -> p v j", j=TABLE)
        rows = qk[:, :, :, :].rearrange("p g a t -> p (g a t)")[:, 0:11 * P].rearrange("p (r c) -> p r c", c=P)
        xnat = yb[:, 0:8, :].rearrange("p k t -> p (k t)").rearrange("p (b d) -> p b d", b=TB)
        UPW = TAPS - 1 + S
        up = scratch[:, 0:3 * UPW].rearrange("p (r w) -> p r w", w=UPW)
        tmp = scratch[:, 900:900 + 4 * S].rearrange("p (r w) -> p r w", w=S)
        accp = scratch[:, 1924:1924 + 2 * S].rearrange("p (r w) -> p r w", w=S)
        acca = scratch[:, 2436:2436 + 2 * S].rearrange("p (r w) -> p r w", w=S)
        sg = scratch[:, 2948:2948 + 2 * S].rearrange("p (r w) -> p r w", w=S)
        sq4 = scratch[:, 3460:3460 + 4 * S].rearrange("p (r w) -> p r w", w=S)
        Lb = scratch[:, 0:6 * 384].rearrange("p (r w) -> p r w", w=384)
        PT = scratch[:, 2304:2304 + 6 * 384].rearrange("p (r w) -> p r w", w=384)
        bank = [ctx.enter_context(nc.psum_tensor(f"bank{i}", [P, 512], F32)) for i in range(8)]
        skew = nc.dram_tensor("skew", (HEADS2, P, TABLE), F32, kind="Internal").ap()

        def norm_g(i, k):
            return cols[:, 8 * i + k:8 * i + k + 1]
        FQ, FK, QK2, POS, ROWB, ROWC = 48, 49, 50, 56, 88, 88 + 96
        def short_w(k, c):
            return cols[:, ROWC + k * KE + c:ROWC + k * KE + c + 1]
        eps = small[:, 0:1]
        gq = small[:, 1:6]
        fb = small[0:FH, 8:9]
        gate_s = small[:, 16:16 + TB * 24].rearrange("p (b n) -> p b n", b=TB)
        mstat = small[:, 64:64 + 18].rearrange("p (r n) -> p r n", r=3)
        nstat = small[:, 84:84 + 18].rearrange("p (r n) -> p r n", r=3)
        sstat = small[:, 104:104 + 18].rearrange("p (r n) -> p r n", r=3)
        fstat = small[:, 124:124 + 18].rearrange("p (r n) -> p r n", r=3)
        jstat = small[:, 144:144 + 12].rearrange("p (r n) -> p r n", r=3)
        best = small[:, 160:160 + 2 * 8].rearrange("p (r n) -> p r n", r=2)
        iw_s = small[:, 180:180 + 8].rearrange("p (b n) -> p b n", b=TB)

        setup_loaded = sem("setup_loaded")
        unit_loaded = [sem(f"unit_loaded{i}") for i in range(RING)]
        unit_done = sem("unit_done")
        set_done = sem("set_done")
        set_used = sem("set_used")
        set_pool = sem("set_pool")
        set_dve = sem("set_dve")
        tab_done = sem("tab_done")
        tab_copied = sem("tab_copied")
        skew_written = sem("skew_written")
        T_loaded = sem("T_loaded")
        cmpw_loaded = sem("cmpw_loaded")
        x_done = sem("x_done")
        sq_done = sem("sq_done")
        ss_done = sem("ss_done")
        std_done = sem("std_done")
        rr_done = sem("rr_done")
        xn_done = sem("xn_done")
        step = sem("dve_step")
        out_stored = sem("out_stored")
        steps = [0]

        def wait(eng, s, value):
            if value > 0:
                eng.wait_ge(s, value)

        def chain(dve, ins):
            steps[0] += 1
            ins.then_inc(step, 1)
            dve.wait_ge(step, steps[0])

        units = []

        def unit_in(w, segments):
            parts, at = [], 0
            for c0, n in segments:
                parts.append((KD, at, n, w[:, c0:c0 + n].rearrange("(k p) n -> p k n", p=P)))
                at += n
            units.append((at, parts))
            return len(units) - 1

        def unit_out(w, k0, nk, d):
            src = w[k0 * P:(k0 + nk) * P, d * P:(d + 1) * P].rearrange("(k p) n -> p k n", p=P)
            units.append((P, [(nk, 0, P, src)]))
            return len(units) - 1

        def slot(u, nk):
            w = units[u][0]
            at = (u % RING) * UNIT
            return ring[:, at:at + nk * w].rearrange("p (k n) -> p k n", n=w)

        groups = []

        def group(free):
            groups.append(free)
            return len(groups) - 1

        def take_bank(pe, g):
            if g >= 2:
                wait(pe, *groups[g - 2])
            return bank[g % 2]

        def wait_unit(pe, u):
            before = sum(len(units[v][1]) for v in range(u % RING, u + 1, RING))
            pe.wait_ge(unit_loaded[u % RING], 16 * before)

        NPH = 6
        def x_free(ph, g):
            return (x_done, 4 * ph + 4 + g + 1)

        def plan_out(ph, w, nk, per):
            got = []
            for g in range(4):
                us = [unit_out(w, k0, per, 2 * g + a) for a in range(2) for k0 in range(0, nk, per)]
                got.append((group(x_free(ph, g)), us))
            return got

        u_done, sg_done, sz_done = sem("u_done"), sem("sg_done"), sem("sz_done")
        tmp_done, tap_done, conv_done = sem("tmp_done"), sem("tap_done"), sem("conv_done")
        mean_done, dc_done, sqd_done, sqm_done = sem("mean_done"), sem("dc_done"), sem("sqd_done"), sem("sqm_done")
        lstd_done, dn_done, act_done, y_done = sem("lstd_done"), sem("dn_done"), sem("act_done"), sem("y_done")
        pad_done = sem("pad_done")

        def plan_conf(ph, j):
            w = t["a_w_in"][j]
            n = {"ph": ph, "j": j}
            n["vg"] = [(group((u_done, j * KE + c + 1)), unit_in(w, [(c * P, P), (E + c * P, P)])) for c in range(KE)]
            n["z"] = [(group((sz_done, j * 8 + i + 1)), unit_in(w, [(2 * E + i * 2 * P, 2 * P)])) for i in range(8)]
            n["out"] = plan_out(ph, t["a_w_out"][j], KE, KE)
            return n

        f_raw, f_sq, f_ss, f_std, f_rr = sem("f_raw"), sem("f_sq"), sem("f_ss"), sem("f_std"), sem("f_rr")
        f_rb, f_n, f_c, f_v, f_z, f_e = sem("f_rb"), sem("f_n"), sem("f_c"), sem("f_v"), sem("f_z"), sem("f_e")

        def plan_fox(ph):
            w = t["b_w_in"][0]
            n = {"ph": ph}
            n["f"] = (group((f_e, 1)), unit_in(w, [(4 * E, FH)]))
            n["qk"] = [(group((f_raw, h + 1)), unit_in(w, [(h * P, P), (E + h * P, P)])) for h in range(FH)]
            n["z"] = [(group((f_z, i + 1)), unit_in(w, [(3 * E + i * 2 * P, 2 * P)])) for i in range(8)]
            n["v"] = [(group((f_v, i + 1)), unit_in(w, [(2 * E + i * 2 * P, 2 * P)])) for i in range(8)]
            n["out"] = plan_out(ph, t["b_w_out"][0], KE, KE)
            return n

        c_cg, c_cu, c_sz, c_y = sem("c_cg"), sem("c_cu"), sem("c_sz"), sem("c_y")

        def plan_short(ph):
            w = t["c_w_in"][0]
            n = {"ph": ph, "uc": [], "bz": []}
            for c in range(KE):
                n["uc"].append((group((c_cu, c + 1)), unit_in(w, [(c * P, P), (2 * E + c * P, P)])))
                n["bz"].append((group((c_y, c + 1)), unit_in(w, [(E + c * P, P), (3 * E + c * P, P)])))
            n["out"] = plan_out(ph, t["c_w_out"][0], KE, KE)
            return n

        m_raw, m_sq, m_ss, m_std, m_rr = sem("m_raw"), sem("m_sq"), sem("m_ss"), sem("m_std"), sem("m_rr")
        m_rb, m_n, m_nat, m_mix = sem("m_rb"), sem("m_n"), sem("m_nat"), sem("m_mix")

        br_used, mix_s, mixed = sem("br_used"), sem("mix_s"), sem("mixed")

        def plan_mixers(ph):
            w = t["w_in_2"][0]
            kv = [OFF_KV + 128 * i for i in range(6)]
            def dup2(c0):
                return [(c0, HD), (c0, HD), (c0 + HD, HD), (c0 + HD, HD)]
            order = [("raw", [(OFF_AK, HD), (OFF_AK, HD), (OFF_IK, HD), (OFF_IK, HD)]),
                     ("raw", [(OFF_IQ, 2 * P)]),
                     ("nat", [(OFF_AV, HD), (kv[3], P), (OFF_IW, IDX_H), (OFF_BG, 3 * B_H)]),
                     ("cmp", dup2(kv[0])), ("cmp", dup2(kv[1]))]
            order += [("raw", [(i * 2 * P, 2 * P)]) for i in range(2)]
            order += [("raw", [(OFF_BQ + i * 2 * P, 2 * P)]) for i in range(2)]
            order += [("raw", dup2(kv[2])), ("raw", dup2(kv[4]))]
            order += [("raw", [(OFF_CQ + i * 2 * P, 2 * P)]) for i in range(3)]
            order += [("raw", [(OFF_CK + i * 2 * P, 2 * P)]) for i in range(3)]
            order += [("nat", [(kv[5], P)])] + [("nat", [(OFF_CV + i * 2 * P, 2 * P)]) for i in range(3)]
            n = {"ph": ph, "in": []}
            for i, (kind, segments) in enumerate(order):
                n["in"].append((kind, group((m_raw, i + 1)), unit_in(w, segments)))
            n["mix"] = [(group((m_mix, i + 1)), unit_in(w, [(OFF_MIX + i * 2 * P, 2 * P)])) for i in range(12)]
            n["br"] = []
            for d in range(0, KD, 2):
                ua = [unit_out(t["w_branch_a_2"][0], 0, 4, d + a) for a in range(2)]
                ub = [unit_out(t["w_branch_b_2"][0], 0, 4, d + a) for a in range(2)]
                uc = [unit_out(t["w_branch_c_2"][0], 0, 2, d + a) for a in range(2)]
                gs = [group((br_used, 3 * (d // 2) + i + 1)) for i in range(3)]
                n["br"].append(list(zip(gs, (ua, ub, uc))))
            n["out"] = plan_out(ph, t["w_out_2"][0], KD, KD)
            return n

        h_silu, h_done = sem("h_silu"), sem("h_done")

        def plan_ffn(ph):
            w = t["w_ffn_in_2"][0]
            n = {"ph": ph}
            n["gu"] = [(group((h_done, i + 1)), unit_in(w, [(i * P, P), (FF + i * P, P)])) for i in range(KF)]
            n["out"] = plan_out(ph, t["w_ffn_out_2"][0], KF, KF // 2)
            return n

        conf0 = plan_conf(0, 0)
        fox = plan_fox(1)
        short = plan_short(2)
        conf1 = plan_conf(3, 1)
        mixers = plan_mixers(4)
        ffn = plan_ffn(5)
        GAIN = [0, 2, 3, 1, 4, 5]

        def rms_act(act, ph):
            for g in range(4):
                act.wait_ge(x_done, 4 * ph + g + 1)
                nc.scalar.activation(sqb[:, 2 * g:2 * g + 2, :], xT[:, 2 * g:2 * g + 2, :], ACT.Square).then_inc(sq_done, 1)
            act.wait_ge(ss_done, ph + 1)
            nc.scalar.activation(std[:, 0:S], bank[7][:, 0:S], ACT.Sqrt, scale=1.0 / D, bias=eps).then_inc(std_done, 1)

        def rms_pe(pe, ph):
            for k in range(KD):
                pe.wait_ge(sq_done, 4 * ph + k // 2 + 1)
                mm = nc.tensor.matmul(bank[7][:, 0:S], ones, sqb[:, k, :], start=(k == 0), stop=(k == KD - 1))
            mm.then_inc(ss_done, 1)

        def rms_dve(dve, ph):
            dve.wait_ge(std_done, ph + 1)
            nc.vector.reciprocal(rr[:, 0:S], std[:, 0:S]).then_inc(rr_done, 1)
            dve.wait_ge(rr_done, ph + 1)
            for k in range(KD):
                nc.vector.scalar_tensor_tensor(xn[:, k, :], xT[:, k, :], norm_g(GAIN[ph], k), rr[:, 0:S],
                                               ALU.mult, ALU.mult).then_inc(xn_done, 1)

        def proj_T(pe, g, u, first=False, ph=0, widths=(P, P)):
            b = take_bank(pe, g)
            wait_unit(pe, u)
            w = slot(u, KD)
            for a, n in enumerate(widths):
                for k in range(KD):
                    if first and a == 0:
                        pe.wait_ge(xn_done, KD * ph + k + 1)
                    mm = nc.tensor.matmul(b[0:n, a * S:(a + 1) * S], w[:, k, a * P:a * P + n], xn[:, k, :],
                                          start=(k == 0), stop=(k == KD - 1))
            mm.then_inc(unit_done, 1)

        def proj_N(pe, g, u):
            b = take_bank(pe, g)
            wait_unit(pe, u)
            n = units[u][0]
            w = slot(u, KD)
            for tb in range(TB):
                for k in range(KD):
                    mm = nc.tensor.matmul(b[:, tb * S:tb * S + n], xn[:, k, tb * P:(tb + 1) * P], w[:, k, :],
                                          start=(k == 0), stop=(k == KD - 1))
            mm.then_inc(unit_done, 1)

        def out_pe(pe, n, src, nk, ready, base=0):
            seen = set()
            for g, us in n["out"]:
                b = take_bank(pe, g)
                per = nk * 2 // len(us)
                for i, u in enumerate(us):
                    wait_unit(pe, u)
                    a, k0 = divmod(i * per, nk)
                    w = slot(u, per)
                    for k in range(per):
                        if k0 + k not in seen:
                            seen.add(k0 + k)
                            pe.wait_ge(ready, base + k0 + k + 1)
                        mm = nc.tensor.matmul(b[:, a * S:(a + 1) * S], w[:, k, :], src[:, k0 + k, :],
                                              start=(k0 + k == 0), stop=(k0 + k == nk - 1))
                    mm.then_inc(unit_done, 1)

        def out_dve(dve, n):
            for i, (g, us) in enumerate(n["out"]):
                dve.wait_ge(unit_done, us[-1] + 1)
                nc.vector.tensor_tensor(xT[:, 2 * i:2 * i + 2, :], bank[g % 2][:, :].rearrange("p (a t) -> p a t", t=S),
                                        xT[:, 2 * i:2 * i + 2, :], ALU.add).then_inc(x_done, 1)

        def conf_act(act, n):
            j = n["j"]
            rms_act(act, n["ph"])
            for c in range(KE):
                g, u = n["vg"][c]
                act.wait_ge(unit_done, u + 1)
                if c >= 2:
                    act.wait_ge(u_done, j * KE + c - 1)
                nc.scalar.activation(sg[:, c % 2, :], bank[g % 2][:, S:2 * S], ACT.Sigmoid).then_inc(sg_done, 1)
                act.wait_ge(u_done, j * KE + c + 1)
                for i in range(TAPS_POOL):
                    k = TAPS_DVE + i
                    m = (j * KE + c) * TAPS_POOL + i
                    wait(act, tap_done, m - 3)
                    src = up[:, c % 3, k:k + S]
                    bias = cols[:, ROWB + j * KE + c:ROWB + j * KE + c + 1] if i == 0 else 0.0
                    nc.scalar.activation(tmp[:, m % 4, :], src, ACT.Identity, scale=taps[:, j, k, c:c + 1],
                                         bias=bias).then_inc(tmp_done, 1)
            for i, (g, u) in enumerate(n["z"]):
                act.wait_ge(unit_done, u + 1)
                nc.scalar.activation(zb[:, 2 * i:2 * i + 2, :], bank[g % 2][:, :].rearrange("p (a t) -> p a t", t=S),
                                     ACT.Silu).then_inc(sz_done, 1)
            for c in range(KE):
                act.wait_ge(dc_done, j * KE + c + 1)
                if c >= 4:
                    act.wait_ge(sqm_done, j * KE + c - 3)
                nc.scalar.activation(sq4[:, c % 4, :], yb[:, c, :], ACT.Square).then_inc(sqd_done, 1)
            act.wait_ge(sqm_done, j * KE + KE)
            nc.scalar.activation(std[:, 0:S], bank[6][:, 0:S], ACT.Sqrt, scale=1.0 / E, bias=eps).then_inc(lstd_done, 1)
            for c in range(KE):
                act.wait_ge(dn_done, j * KE + c + 1)
                lg = cols[:, ROWB + 32 + j * KE + c:ROWB + 32 + j * KE + c + 1]
                lb = cols[:, ROWB + 64 + j * KE + c:ROWB + 64 + j * KE + c + 1]
                nc.scalar.activation(yb[:, c, :], yb[:, c, :], ACT.Silu, scale=lg, bias=lb).then_inc(act_done, 1)

        def conf_pool(pool, n):
            j = n["j"]
            for c in range(KE):
                for i in range(1, TAPS_POOL):
                    m = (j * KE + c) * TAPS_POOL + i
                    pool.wait_ge(tmp_done, m + 1)
                    if i == 1 and c >= 2:
                        pool.wait_ge(conv_done, j * KE + c - 1)
                    a = tmp[:, (m - 1) % 4, :] if i == 1 else accp[:, c % 2, :]
                    if i > 1:
                        pool.wait_ge(tap_done, m)
                    nc.gpsimd.tensor_tensor(accp[:, c % 2, :], a, tmp[:, m % 4, :], ALU.add)\
                        .then_inc(tap_done, 2 if i == 1 else 1)
            for c in range(KE):
                pool.wait_ge(act_done, j * KE + c + 1)
                wait(pool, sz_done, j * 8 + c // 2 + 1)
                nc.gpsimd.tensor_tensor(yb[:, c, :], yb[:, c, :], zb[:, c, :], ALU.mult).then_inc(y_done, 1)

        def conf_dve(dve, n):
            j = n["j"]
            for r in range(3):
                nc.vector.memset(up[:, r, 0:TAPS - 1], 0.0).then_inc(pad_done, 1)
            dve.wait_ge(pad_done, 3 * j + 3)
            rms_dve(dve, n["ph"])
            for c in range(KE):
                g, u = n["vg"][c]
                dve.wait_ge(sg_done, j * KE + c + 1)
                if c >= 3:
                    wait(dve, tmp_done, (j * KE + c - 2) * TAPS_POOL)
                nc.vector.tensor_tensor(up[:, c % 3, TAPS - 1:UPW], bank[g % 2][:, 0:S], sg[:, c % 2, :],
                                        ALU.mult).then_inc(u_done, 1)
                dve.wait_ge(u_done, j * KE + c + 1)
                prev = [None, None]
                for k in range(TAPS_DVE):
                    a = k % 2
                    src = up[:, c % 3, k:k + S]
                    w = taps[:, j, k, c:c + 1]
                    if prev[a] is None:
                        ins = nc.vector.tensor_scalar(acca[:, a, :], src, w, None, ALU.mult)
                    else:
                        dve.wait_ge(step, prev[a])
                        ins = nc.vector.scalar_tensor_tensor(acca[:, a, :], src, w, acca[:, a, :], ALU.mult, ALU.add)
                    steps[0] += 1
                    ins.then_inc(step, 1)
                    prev[a] = steps[0]
                dve.wait_ge(step, steps[0])
                chain(dve, nc.vector.tensor_tensor(acca[:, 0, :], acca[:, 0, :], acca[:, 1, :], ALU.add))
                dve.wait_ge(tap_done, (j * KE + c + 1) * TAPS_POOL)
                nc.vector.tensor_tensor(yb[:, c, :], acca[:, 0, :], accp[:, c % 2, :], ALU.add).then_inc(conv_done, 1)
                dve.wait_ge(conv_done, j * KE + c + 1)
            dve.wait_ge(mean_done, j + 1)
            for c in range(KE):
                nc.vector.scalar_tensor_tensor(yb[:, c, :], bank[7][:, 0:S], -1.0 / E, yb[:, c, :],
                                               ALU.mult, ALU.add).then_inc(dc_done, 1)
            dve.wait_ge(lstd_done, j + 1)
            chain(dve, nc.vector.reciprocal(rr[:, 0:S], std[:, 0:S]))
            for c in range(KE):
                nc.vector.tensor_tensor(yb[:, c, :], yb[:, c, :], rr[:, 0:S], ALU.mult).then_inc(dn_done, 1)
            out_dve(dve, n)

        def conf_pe(pe, n):
            j = n["j"]
            rms_pe(pe, n["ph"])
            for c, (g, u) in enumerate(n["vg"]):
                proj_T(pe, g, u, c == 0, n["ph"])
            for i, (g, u) in enumerate(n["z"]):
                proj_T(pe, g, u)
                for c in (2 * i, 2 * i + 1):
                    pe.wait_ge(conv_done, j * KE + c + 1)
                    mm = nc.tensor.matmul(bank[7][:, 0:S], ones, yb[:, c, :], start=(c == 0), stop=(c == KE - 1))
            mm.then_inc(mean_done, 1)
            for c in range(KE):
                pe.wait_ge(sqd_done, j * KE + c + 1)
                nc.tensor.matmul(bank[6][:, 0:S], ones, sq4[:, c % 4, :], start=(c == 0),
                                 stop=(c == KE - 1)).then_inc(sqm_done, 1)
            out_pe(pe, n, yb, KE, y_done, j * KE)

        class Jobs:
            def __init__(self, name, jobs):
                self.jobs = jobs
                self.first = [sum(len(x["parts"]) for x in jobs[:i]) for i in range(len(jobs) + 1)]
                self.s_ready = sem(f"{name}_logits_ready")
                self.ttr_done = sem(f"{name}_bias_added")
                self.nm_done = sem(f"{name}_max_ready")
                self.exp_done = sem(f"{name}_exp_done")
                self.norm_done = sem(f"{name}_probs_ready")
                self.tr_done = sem(f"{name}_probs_transposed")
                self.pt_copied = sem(f"{name}_transposes_copied")
                self.pv_done = sem(f"{name}_values_summed")
                self.o_done = sem(f"{name}_output_used")

        BLOCKS = ((0, P), (P, 3 * P))

        def spans(part):
            return ((0, NCMP), (P, P + NCMP)) if part.get("cmp") else BLOCKS

        def qk_pe(pe, A, j, ready=None):
            job = A.jobs[j]
            for s, v in job.get("waits", []):
                pe.wait_ge(s, v)
            for i, part in enumerate(job["parts"]):
                p = A.first[j] + i
                wait(pe, A.ttr_done, 2 * (p - 1))
                b = bank[2 + p % 2]
                for tb, (c0, c1) in enumerate(spans(part)):
                    prods = [(part["q"][:, tb * P:(tb + 1) * P], part["k"][:, 0:c1 - c0])]
                    prods += [(l(tb), r(tb)) for l, r in part.get("more", [])]
                    for m, (l, r) in enumerate(prods):
                        mm = nc.tensor.matmul(b[:, c0:c1], l, r, start=(m == 0), stop=(m == len(prods) - 1))
                mm.then_inc(A.s_ready, 1)

        def scores_dve(dve, A, j):
            job = A.jobs[j]
            r = j % 3
            for i, part in enumerate(job["parts"]):
                p = A.first[j] + i
                dve.wait_ge(A.s_ready, p + 1)
                wait(dve, A.tr_done, p - 5)
                for tb, (c0, c1) in enumerate(spans(part)):
                    nc.vector.tensor_tensor_reduce(Lb[:, p % 6, c0:c1], bank[2 + p % 2][:, c0:c1], part["bias"](tb), 1.0,
                                                   -3.0e38, ALU.add, ALU.max, mstat[:, r, 3 * tb + i:3 * tb + i + 1])\
                        .then_inc(A.ttr_done, 1)
            dve.wait_ge(A.ttr_done, 2 * A.first[j + 1])
            n = len(job["parts"])
            m = mstat[:, r, :].rearrange("p (b i) -> p b i", b=2)[:, :, 0:n]
            d = nstat[:, r, :].rearrange("p (b i) -> p b i", b=2)[:, :, 0:n]
            if job.get("joint"):
                chain(dve, nc.vector.tensor_reduce(jstat[:, r, 0:2], m, AX, ALU.max))
                m, d = jstat[:, r, 0:2], nstat[:, r, 0:2]
            nc.vector.tensor_scalar(d, m, -1.0, 1e29, ALU.mult, ALU.min).then_inc(A.nm_done, 1)

        def exps_act(act, A, j):
            job = A.jobs[j]
            r = j % 3
            act.wait_ge(A.nm_done, j + 1)
            for i, part in enumerate(job["parts"]):
                p = A.first[j] + i
                for tb, (c0, c1) in enumerate(spans(part)):
                    nm = nstat[:, r, tb:tb + 1] if job.get("joint") else nstat[:, r, 3 * tb + i:3 * tb + i + 1]
                    nc.scalar.activation(Lb[:, p % 6, c0:c1], Lb[:, p % 6, c0:c1], ACT.Exp, bias=nm, scale=1.0,
                                         accum_out=sstat[:, r, 3 * tb + i:3 * tb + i + 1]).then_inc(A.exp_done, 1)

        def norm_dve(dve, A, j):
            job = A.jobs[j]
            r = j % 3
            n = len(job["parts"])
            dve.wait_ge(A.exp_done, 2 * A.first[j + 1])
            s = sstat[:, r, :].rearrange("p (b i) -> p b i", b=2)[:, :, 0:n]
            f = fstat[:, r, :].rearrange("p (b i) -> p b i", b=2)[:, :, 0:n]
            if job.get("joint"):
                chain(dve, nc.vector.tensor_reduce(jstat[:, r, 2:4], s, AX, ALU.add))
                s, f = jstat[:, r, 2:4], fstat[:, r, 0:2]
            chain(dve, nc.vector.tensor_scalar(s, s, 1e-30, None, ALU.max))
            chain(dve, nc.vector.reciprocal(f, s))
            if job.get("gate") is not None:
                chain(dve, nc.vector.tensor_tensor(f, f, job["gate"], ALU.mult))
            for i, part in enumerate(job["parts"]):
                p = A.first[j] + i
                for tb, (c0, c1) in enumerate(spans(part)):
                    fac = fstat[:, r, tb:tb + 1] if job.get("joint") else fstat[:, r, 3 * tb + i:3 * tb + i + 1]
                    nc.vector.tensor_scalar(Lb[:, p % 6, c0:c1], Lb[:, p % 6, c0:c1], fac, None, ALU.mult)\
                        .then_inc(A.norm_done, 1)

        def tr_pe(pe, A, j):
            for i, part in enumerate(A.jobs[j]["parts"]):
                p = A.first[j] + i
                pe.wait_ge(A.norm_done, 2 * p + 2)
                wait(pe, A.pt_copied, p - 1)
                b = bank[4 + p % 2]
                if part.get("cmp"):
                    for tb in range(TB):
                        mm = nc.tensor.transpose(b[0:NCMP, tb * P:(tb + 1) * P], Lb[:, p % 6, tb * P:tb * P + NCMP], ident)
                else:
                    for m in range(3):
                        mm = nc.tensor.transpose(b[:, m * P:(m + 1) * P], Lb[:, p % 6, m * P:(m + 1) * P], ident)
                mm.then_inc(A.tr_done, 1)

        def pt_act(act, A, j):
            for i, part in enumerate(A.jobs[j]["parts"]):
                p = A.first[j] + i
                act.wait_ge(A.tr_done, p + 1)
                wait(act, A.pv_done, p - 5)
                rows_, w = (NCMP, S) if part.get("cmp") else (P, 3 * P)
                nc.scalar.copy(PT[0:rows_, p % 6, 0:w], bank[4 + p % 2][0:rows_, 0:w]).then_inc(A.pt_copied, 1)

        def pv_pe(pe, A, j):
            job = A.jobs[j]
            tile, half, mw = job["tile"], job["half"], job["width"]
            for s, v in job.get("v_waits", []):
                pe.wait_ge(s, v)
            if half == 0:
                wait(pe, A.o_done, tile - 1)
            o = bank[6 + tile % 2][64 * half:64 * half + mw, :]
            n = len(job["parts"])
            for i, part in enumerate(job["parts"]):
                p = A.first[j] + i
                pe.wait_ge(A.pt_copied, p + 1)
                if part.get("cmp"):
                    mm = nc.tensor.matmul(o[:, 0:S], part["v"](0), PT[0:NCMP, p % 6, 0:S], start=(i == 0), stop=(i == n - 1))
                else:
                    nc.tensor.matmul(o[:, 0:S], part["v"](0), PT[:, p % 6, 0:S], start=(i == 0), stop=False)
                    mm = nc.tensor.matmul(o[:, P:S], part["v"](1), PT[:, p % 6, S:S + P], start=False, stop=(i == n - 1))
                mm.then_inc(A.pv_done, 1)

        fw = sg[0:FH, :, :]
        ssr = std[0:FH, :]

        c_pos = sb("c_pos", 2 * S, FH)
        cpos, cneg = c_pos[:, 0:S], c_pos[:, S:2 * S]

        def sel_h(h, n):
            return ident[0:FH, h:h + 1].to_broadcast((FH, n))

        fox_jobs = []
        for h in range(FH):
            part = {"q": qk[:, h, 0, :], "k": qk[:, h, 1, :],
                    "more": [(lambda tb, h=h: sel_h(h, P), lambda tb: cneg[:, 0:(tb + 1) * P]),
                             (lambda tb: cpos[:, tb * P:(tb + 1) * P], lambda tb, h=h: sel_h(h, (tb + 1) * P))],
                    "bias": lambda tb: cst[:, C_MASK + P:C_MASK + S] if tb == 0 else cst[:, C_MASK:C_MASK + S],
                    "v": lambda sblk, h=h: vb[:, sblk, h * P:(h + 1) * P]}
            fox_jobs.append({"parts": [part], "tile": h, "half": 0, "width": P, "waits": [],
                             "v_waits": [(f_v, h // 2 + 1)]})
        fox_jobs[0]["waits"] = [(f_c, 4), (f_n, 2 * FH)]
        AF = Jobs("fox", fox_jobs)
        fsq = [scratch[:, 900 + 512 * i:900 + 512 * i + 512] for i in range(2)]

        def fox_act(act, n):
            rms_act(act, n["ph"])
            g, u = n["f"]
            act.wait_ge(unit_done, u + 1)
            nc.scalar.activation(fw[:, 0, :], bank[g % 2][0:FH, 0:S], ACT.Identity, bias=fb).then_inc(f_e, 1)
            act.wait_ge(f_e, 1)
            nc.scalar.activation(fw[:, 1, :], fw[:, 0, :], ACT.Abs).then_inc(f_e, 1)
            act.wait_ge(f_e, 2)
            nc.scalar.activation(fw[:, 1, :], fw[:, 1, :], ACT.Exp, scale=-1.0).then_inc(f_e, 1)
            act.wait_ge(f_e, 3)
            nc.scalar.activation(fw[:, 1, :], fw[:, 1, :], ACT.Ln, bias=1.0).then_inc(f_e, 1)
            for h, (g, u) in enumerate(n["qk"]):
                act.wait_ge(unit_done, u + 1)
                wait(act, f_ss, h - 1)
                nc.scalar.activation(fsq[h % 2], bank[g % 2][:, :], ACT.Square).then_inc(f_sq, 1)
                nc.scalar.copy(qk[:, h, :, :].rearrange("p a t -> p (a t)"), bank[g % 2][:, :]).then_inc(f_raw, 1)
            act.wait_ge(f_ss, FH)
            nc.scalar.activation(ssr, bank[7][0:FH, :], ACT.Sqrt, scale=1.0 / FD, bias=eps[0:FH, :]).then_inc(f_std, 1)
            for i, (g, u) in enumerate(n["z"]):
                act.wait_ge(unit_done, u + 1)
                nc.scalar.activation(zb[:, 2 * i:2 * i + 2, :], bank[g % 2][:, :].rearrange("p (a t) -> p a t", t=S),
                                     ACT.Silu).then_inc(f_z, 1)
            for j in range(FH + 1):
                if j < FH:
                    exps_act(act, AF, j)
                    if j % 2 == 0:
                        i = j // 2
                        g, u = n["v"][i]
                        act.wait_ge(unit_done, u + 1)
                        nc.scalar.copy(vb[:, :, i * S:(i + 1) * S], bank[g % 2][:, :].rearrange("p (b n) -> p b n", b=TB))\
                            .then_inc(f_v, 1)
                if j >= 1:
                    pt_act(act, AF, j - 1)

        def fox_dve(dve, n):
            rms_dve(dve, n["ph"])
            dve.wait_ge(f_e, 4)
            nc.vector.scalar_tensor_tensor(cpos, fw[:, 0, :], 0.0, fw[:, 1, :], ALU.min, ALU.subtract).then_inc(f_c, 1)
            dve.wait_ge(f_c, 1)
            nc.vector.tensor_tensor_scan(cneg, ones[0:FH, 0:1].to_broadcast((FH, S)), cpos, 0.0, ALU.mult, ALU.add).then_inc(f_c, 1)
            dve.wait_ge(f_c, 2)
            nc.vector.tensor_copy(cpos, cneg).then_inc(f_c, 1)
            dve.wait_ge(f_c, 3)
            nc.vector.tensor_scalar(cneg, cneg, -1.0, None, ALU.mult).then_inc(f_c, 1)
            dve.wait_ge(f_std, 1)
            nc.vector.reciprocal(rr[0:FH, :], ssr).then_inc(f_rr, 1)
            for h in range(FH):
                dve.wait_ge(f_rb, h + 1)
                for a in range(2):
                    gain = gq[:, 0:1] if a == 0 else cols[:, FK:FK + 1]
                    nc.vector.scalar_tensor_tensor(qk[:, h, a, :], qk[:, h, a, :], gain, bank[2 + h % 2][:, a * S:(a + 1) * S],
                                                   ALU.mult, ALU.mult).then_inc(f_n, 1)
            for j in range(FH + 2):
                if j < FH:
                    scores_dve(dve, AF, j)
                if 1 <= j <= FH:
                    norm_dve(dve, AF, j - 1)
                if j >= 2:
                    h = j - 2
                    dve.wait_ge(AF.pv_done, h + 1)
                    nc.vector.tensor_tensor(yb[:, h, :], bank[6 + h % 2][:, 0:S], zb[:, h, :], ALU.mult).then_inc(AF.o_done, 1)
            out_dve(dve, n)

        def fox_pe(pe, n):
            rms_pe(pe, n["ph"])
            g, u = n["f"]
            proj_T(pe, g, u, True, n["ph"], (FH,))

            def sums(h):
                pe.wait_ge(f_sq, h + 1)
                nc.tensor.matmul(bank[7][0:FH, :], cst[:, C_E1 + 15 - h:C_E1 + 15 - h + FH], fsq[h % 2],
                                 start=(h == 0), stop=(h == FH - 1)).then_inc(f_ss, 1)

            for h, (g, u) in enumerate(n["qk"]):
                proj_T(pe, g, u)
                if h >= 1:
                    sums(h - 1)
            proj_T(pe, *n["z"][0])
            sums(FH - 1)
            for i in range(1, 8):
                proj_T(pe, *n["z"][i])
                if i >= 2:
                    for h in range(3 * (i - 2), min(3 * (i - 1), FH)):
                        fox_rb(pe, h)
            for j in range(FH + 2):
                if j < FH:
                    qk_pe(pe, AF, j)
                    if j % 2 == 0:
                        proj_N(pe, *n["v"][j // 2])
                if 1 <= j <= FH:
                    tr_pe(pe, AF, j - 1)
                if j >= 2:
                    pv_pe(pe, AF, j - 2)
            out_pe(pe, n, yb, KE, AF.o_done)

        def fox_rb(pe, h):
            if h == 0:
                pe.wait_ge(f_rr, 1)
            wait(pe, f_n, 2 * (h - 1))
            nc.tensor.matmul(bank[2 + h % 2][:, :], sel_h(h, P), rr[0:FH, :], start=True, stop=True).then_inc(f_rb, 1)

        cup = scratch[:, 0:2 * (S + 2)].rearrange("p (r w) -> p r w", w=S + 2)
        ccg = scratch[:, 600:600 + 2 * S].rearrange("p (r w) -> p r w", w=S)
        csz = scratch[:, 1200:1200 + 2 * S].rearrange("p (r w) -> p r w", w=S)
        cac = scratch[:, 1800:1800 + 2 * S].rearrange("p (r w) -> p r w", w=S)

        def short_act(act, n):
            rms_act(act, n["ph"])
            for c in range(KE):
                g, u = n["uc"][c]
                act.wait_ge(unit_done, u + 1)
                wait(act, c_cu, c - 1)
                nc.scalar.copy(ccg[:, c % 2, :], bank[g % 2][:, S:2 * S]).then_inc(c_cg, 1)
                g, u = n["bz"][c]
                act.wait_ge(unit_done, u + 1)
                wait(act, c_y, c - 1)
                nc.scalar.activation(csz[:, c % 2, :], bank[g % 2][:, S:2 * S], ACT.Silu).then_inc(c_sz, 1)

        def short_dve(dve, n):
            for r in range(2):
                chain(dve, nc.vector.memset(cup[:, r, 0:2], 0.0))
            rms_dve(dve, n["ph"])
            for c in range(KE):
                g, u = n["uc"][c]
                dve.wait_ge(c_cg, c + 1)
                nc.vector.tensor_tensor(cup[:, c % 2, 2:S + 2], bank[g % 2][:, 0:S], ccg[:, c % 2, :], ALU.mult).then_inc(c_cu, 1)
                dve.wait_ge(c_cu, c + 1)
                chain(dve, nc.vector.tensor_scalar(cac[:, c % 2, :], cup[:, c % 2, 0:S], short_w(0, c), None, ALU.mult))
                for k in range(1, SHORT):
                    chain(dve, nc.vector.scalar_tensor_tensor(cac[:, c % 2, :], cup[:, c % 2, k:k + S], short_w(k, c),
                                                              cac[:, c % 2, :], ALU.mult, ALU.add))
                g, u = n["bz"][c]
                dve.wait_ge(c_sz, c + 1)
                chain(dve, nc.vector.tensor_tensor(cac[:, c % 2, :], cac[:, c % 2, :], csz[:, c % 2, :], ALU.mult))
                nc.vector.tensor_tensor(yb[:, c, :], bank[g % 2][:, 0:S], cac[:, c % 2, :], ALU.mult).then_inc(c_y, 1)
            out_dve(dve, n)

        def short_pe(pe, n):
            rms_pe(pe, n["ph"])
            for c in range(KE):
                proj_T(pe, *n["uc"][c], c == 0, n["ph"])
                proj_T(pe, *n["bz"][c])
            out_pe(pe, n, yb, KE, c_y)

        msq = [scratch[:, 2304 + 512 * i:2304 + 512 * i + 512] for i in range(2)]
        RAW_OF = {}
        for i, (kind, g, u) in enumerate(mixers["in"]):
            if kind == "raw":
                RAW_OF[i] = len(RAW_OF)
        normed = [i for i in RAW_OF if i != 1]
        IK, IQ = qk[:, 0, 1, :], qk[:, 1, :, :]
        AQ, BQ, KS, KW, CQ, CK = 2, 4, 6, 7, 8, 11
        V_A, V_S, V_IW, V_BG, V_W, V_C = 0, HD, HD + P, HD + P + IDX_H, 220, 348
        NAT_AT = {2: 0, 17: V_W, 18: V_C, 19: V_C + S, 20: V_C + 2 * S}
        vflat = vb_flat[:, 0:TB * 1116].rearrange("p (b n) -> p b n", b=TB)
        rest = vb_flat[:, TB * 1116:TB * E]
        cmp_in = rest[:, 0:2 * S].rearrange("p (g t) -> p g t", g=B_G)
        cblk = [rest[:, 512 + 480 * i:512 + 480 * (i + 1)].rearrange("p (l g n) -> p l g n", l=LC, g=B_G) for i in range(2)]
        kcT = rest[:, 1472:1502]
        vcT = rest[:, 1502:1532]
        vcN = rest[0:NCMP, 1532:1532 + 2 * HD].rearrange("p (g e) -> p g e", g=B_G)
        kraw, ksq = rest[:, 1660:1690], rest[:, 1690:1720]
        kstd = rest[:, 1720:1750]
        cw = mix[:, 0:12, :].rearrange("p k t -> p (k t)")
        cwk = cw[:, 0:LC * P].rearrange("p (l e) -> p l e", l=LC)
        cwv = cw[:, LC * P:LC * P + LC * HD].rearrange("p (l e) -> p l e", l=LC)
        keep = mix[:, 14:18, :].rearrange("p k t -> p (k t)")
        isc = keep[:, 0:384]
        rel4 = keep[:, 384:384 + 512].rearrange("p (r w) -> p r w", w=256)
        amask = sb("amask", 384)
        i_s, i_r, i_a, i_top, i_m = sem("i_s"), sem("i_r"), sem("i_a"), sem("i_top"), sem("i_m")
        k_in, k_blk, k_mm, k_c, k_v, k_sq = sem("k_in"), sem("k_blk"), sem("k_mm"), sem("k_c"), sem("k_v"), sem("k_sq")
        k_fin = sem("k_fin")
        g_s = sem("g_s")

        def q_of(s0, h):
            half = h % 2
            return qk[64 * half:64 * half + 64, s0 + h // 4, (h // 2) % 2, :]

        def half_of(ap3, h):
            return ap3[64 * (h % 2):64 * (h % 2) + 64]

        def bias_of(h):
            return lambda tb: T[:, h, P:S] if tb == 0 else T[:, h, :]

        jobs = []
        for hh in range(C_SLOTS):
            parts = []
            for gi in range(3):
                h = gi * C_SLOTS + hh
                parts.append({"q": q_of(CQ, h), "k": q_of(CK, h), "bias": bias_of(A_H + B_H + h),
                              "v": lambda sblk, h=h: vflat[:, sblk, V_C + h * HD:V_C + (h + 1) * HD]})
            jobs.append({"parts": parts, "joint": True, "tile": hh // 2, "half": hh % 2, "width": HD})
        for h in range(B_H):
            g = h // (B_H // B_G)
            parts = [{"cmp": True, "q": q_of(BQ, h), "k": half_of(kcT, h)[:, g * NCMP:(g + 1) * NCMP],
                      "bias": lambda tb: cst[:, C_CMP + tb * NCMP:C_CMP + (tb + 1) * NCMP],
                      "v": lambda sblk, g=g: vcN[:, g, :]},
                     {"q": q_of(BQ, h), "k": half_of(qk[:, KS, g, :], h), "bias": bias_of(A_H + h),
                      "v": lambda sblk, g=g: vflat[:, sblk, V_S + g * HD:V_S + (g + 1) * HD]},
                     {"q": q_of(BQ, h), "k": half_of(qk[:, KW, g, :], h), "bias": bias_of(A_H + h),
                      "v": lambda sblk, g=g: vflat[:, sblk, V_W + g * HD:V_W + (g + 1) * HD]}]
            jobs.append({"parts": parts, "gate": gate_s[:, :, 3 * h:3 * h + 3], "tile": 2 + h // 2, "half": h % 2, "width": HD})
        for h in range(A_H):
            part = {"q": q_of(AQ, h), "k": half_of(qk[:, 0, 0, :], h), "bias": bias_of(h),
                    "more": [(lambda tb: ident, lambda tb: amask[:, 0:P] if tb == 0 else amask[:, P:3 * P])],
                    "v": lambda sblk: vflat[:, sblk, V_A:V_A + HD]}
            jobs.append({"parts": [part], "tile": 6 + h // 2, "half": h % 2, "width": HD})
        NJ = len(jobs)
        jobs[0]["waits"] = [(m_n, NORMED), (T_loaded, 16)]
        jobs[C_SLOTS]["waits"] = [(k_fin, 1)]
        jobs[C_SLOTS]["v_waits"] = [(k_v, 3)]
        jobs[C_SLOTS + B_H]["waits"] = [(i_m, 2)]
        AM = Jobs("m", jobs)

        def filler_at(j):
            per = [1] * NJ
            at = [sum(per[:i]) * 12 // NJ for i in range(NJ + 1)]
            return range(at[j], at[j + 1])

        def mixers_act(act, n):
            rms_act(act, n["ph"])
            act.wait_ge(skew_written, 16 * 4)
            act.dma_start(T[:, :, :], bass.AP(tensor=skew.tensor, offset=skew.offset + P - 1,
                                              ap=[[TABLE - 1, P], [P * TABLE, HEADS2], [1, S]])).then_inc(T_loaded, 16)
            w0 = t["nsa_cmp_w_2"][0]
            for i in range(2):
                act.dma_start(cwk[:, :, i * HD:(i + 1) * HD], w0[0].rearrange("(l q) d e -> (q d) l e", q=2)).then_inc(cmpw_loaded, 16)
            act.dma_start(cwv, w0[1].rearrange("(l q) d e -> (q d) l e", q=2)).then_inc(cmpw_loaded, 16)
            count = {"sq": 0, "cmp": 0}
            for i, (kind, g, u) in enumerate(n["in"]):
                b = bank[g % 2]
                act.wait_ge(unit_done, u + 1)
                if kind == "raw":
                    if i in normed:
                        q = count["sq"]
                        wait(act, m_ss, q - 1)
                        nc.scalar.activation(msq[q % 2], b[:, :], ACT.Square).then_inc(m_sq, 1)
                        count["sq"] += 1
                    nc.scalar.copy(qk[:, RAW_OF[i], :, :].rearrange("p a t -> p (a t)"), b[:, :]).then_inc(m_raw, 1)
                elif kind == "nat":
                    wn = units[u][0]
                    src = b[:, :].rearrange("p (b n) -> p b n", b=TB)[:, :, 0:wn]
                    nc.scalar.copy(vflat[:, :, NAT_AT[i]:NAT_AT[i] + wn], src).then_inc(m_raw, 1)
                else:
                    q = count["cmp"]
                    wait(act, k_blk, q)
                    bb = b[:, :].rearrange("p (g t) -> p g t", g=B_G)
                    nc.scalar.copy(cmp_in[0:64, :, :], bb[0:64, :, :]).then_inc(k_in, 1)
                    nc.scalar.copy(cmp_in[64:P, :, 0:S - 1], bb[64:P, :, 1:S]).then_inc(m_raw, 1)
                    count["cmp"] += 1
                if i == 2:
                    act.wait_ge(m_raw, 3)
                    nc.scalar.activation(gate_s, vflat[:, :, V_BG:V_BG + 24], ACT.Sigmoid).then_inc(g_s, 1)
                if 5 <= i < 9:
                    for m in range(2 * (i - 5), 2 * (i - 4)):
                        act.wait_ge(i_s, m + 1)
                        wait(act, i_a, m - 1)
                        w = P * (m // 4 + 1)
                        nc.scalar.activation(rel4[:, m % 2, 0:w], bank[2 + m % 2][:, 0:w], ACT.Relu).then_inc(i_r, 1)
                if i == 9:
                    act.wait_ge(k_mm, 1)
                    nc.scalar.copy(kraw, bank[4][:, 0:30]).then_inc(k_c, 1)
                    nc.scalar.activation(ksq, bank[4][:, 0:30], ACT.Square).then_inc(k_c, 1)
                    act.wait_ge(k_mm, 2)
                    nc.scalar.copy(vcT[0:64, :], bank[5][0:64, 0:30]).then_inc(k_v, 1)
                if i == 11:
                    for g2 in range(2):
                        act.wait_ge(k_mm, 5)
                        nc.scalar.copy(vcN[:, g2, :], bank[5][0:NCMP, 64 + 64 * g2:128 + 64 * g2]).then_inc(k_v, 1)
            act.wait_ge(m_ss, NORMED)
            nc.scalar.activation(std[0:32, :], bank[7][0:32, :], ACT.Sqrt, scale=1.0 / HD, bias=eps[0:32, :]).then_inc(m_std, 1)
            nc.scalar.activation(kstd, bank[4][:, 64:94], ACT.Sqrt, scale=1.0 / HD, bias=eps).then_inc(m_std, 1)
            for j in range(NJ + 1):
                if j < NJ:
                    exps_act(act, AM, j)
                    for f in filler_at(j):
                        g, u = n["mix"][f]
                        act.wait_ge(unit_done, u + 1)
                        nc.scalar.copy(mix[:, 2 * f:2 * f + 2, :], bank[g % 2][:, :].rearrange("p (a t) -> p a t", t=S)).then_inc(m_mix, 1)
                if j >= 1:
                    pt_act(act, AM, j - 1)
            act.wait_ge(m_mix, 12)
            for d in range(0, KD, 2):
                for i in range(3):
                    nc.scalar.activation(mix[:, 8 * i + d:8 * i + d + 2, :], mix[:, 8 * i + d:8 * i + d + 2, :],
                                         ACT.Sigmoid).then_inc(mix_s, 1)

        def mixers_dve(dve, n):
            rms_dve(dve, n["ph"])
            for q in range(2):
                dve.wait_ge(m_raw, 4 + q)
                src = bass_view(cmp_in)
                pos = cols[:, POS + LC * q:POS + LC * (q + 1)]
                for g in range(B_G):
                    i = nc.vector.tensor_tensor(cblk[q][:, :, g, :].rearrange("p l n -> p n l"), src[g],
                                                pos.unsqueeze(1).to_broadcast((P, NCMP, LC)), ALU.add)
                    if g == 0:
                        chain(dve, i)
                    else:
                        i.then_inc(k_blk, 1)
            for m in range(8):
                tb, h = divmod(m, IDX_H)
                w = P * (tb + 1)
                at = isc[:, 0:P] if tb == 0 else isc[:, P:3 * P]
                dve.wait_ge(i_r, m + 1)
                if h:
                    dve.wait_ge(i_a, m)
                if h == 0:
                    nc.vector.tensor_scalar(at, rel4[:, m % 2, 0:w], vflat[:, tb, V_IW:V_IW + 1], None, ALU.mult).then_inc(i_a, 1)
                else:
                    nc.vector.scalar_tensor_tensor(at, rel4[:, m % 2, 0:w], vflat[:, tb, V_IW + h:V_IW + h + 1], at,
                                                   ALU.mult, ALU.add).then_inc(i_a, 1)
            dve.wait_ge(i_a, 8)
            for tb in range(TB):
                at = isc[:, 0:P] if tb == 0 else isc[:, P:3 * P]
                mk = cst[:, C_MASK + P:C_MASK + S] if tb == 0 else cst[:, C_MASK:C_MASK + S]
                nc.vector.tensor_tensor(at, at, mk, ALU.add).then_inc(i_a, 1)
            dve.wait_ge(i_a, 10)
            done = [0, 0]
            cnt = 0
            for r in range(TOPK // 8):
                for tb in range(TB):
                    at = isc[:, 0:P] if tb == 0 else isc[:, P:3 * P]
                    wait(dve, i_top, done[tb])
                    nc.vector.max(best[:, tb, :], at).then_inc(i_top, 1)
                    cnt += 1
                    done[tb] = cnt
                for tb in range(TB):
                    at = isc[:, 0:P] if tb == 0 else isc[:, P:3 * P]
                    wait(dve, i_top, done[tb])
                    nc.vector.match_replace(at, best[:, tb, :], at, -3.0e38).then_inc(i_top, 1)
                    cnt += 1
                    done[tb] = cnt
            dve.wait_ge(i_top, cnt)
            for tb in range(TB):
                at = slice(0, P) if tb == 0 else slice(P, 3 * P)
                nc.vector.tensor_scalar(amask[:, at], isc[:, at], -2.0e38, NEG, ALU.is_gt, ALU.mult).then_inc(i_m, 1)
            dve.wait_ge(m_std, 1)
            nc.vector.reciprocal(rr[0:32, :], std[0:32, :]).then_inc(m_rr, 1)
            dve.wait_ge(m_std, 2)
            chain(dve, nc.vector.reciprocal(kstd, kstd))
            dve.wait_ge(k_c, 2)
            nc.vector.scalar_tensor_tensor(kcT, kraw, cols[:, QK2 + 3:QK2 + 4], kstd, ALU.mult, ALU.mult).then_inc(k_fin, 1)
            for q, i in enumerate(normed):
                dve.wait_ge(m_rb, q + 1)
                s0 = RAW_OF[i]
                gain = {0: cols[:, QK2 + 1:QK2 + 2], AQ: gq[:, 1:2], BQ: gq[:, 2:3], KS: cols[:, QK2 + 3:QK2 + 4],
                        CQ: gq[:, 3:4], CK: cols[:, QK2 + 5:QK2 + 6]}
                gcol = gain[0 if s0 == 0 else AQ if s0 < BQ else BQ if s0 < KS else KS if s0 < CQ else CQ if s0 < CK else CK]
                wd = S if s0 == 0 else 2 * S
                flat = qk[:, s0, :, :].rearrange("p a t -> p (a t)")[:, 0:wd]
                nc.vector.scalar_tensor_tensor(flat, flat, gcol, bank[2 + q % 2][:, 0:wd], ALU.mult, ALU.mult).then_inc(m_n, 1)
            dve.wait_ge(g_s, 1)
            for j in range(NJ + 2):
                if j < NJ:
                    scores_dve(dve, AM, j)
                if 1 <= j <= NJ:
                    norm_dve(dve, AM, j - 1)
                if j >= 2 and jobs[j - 2]["half"] == 1:
                    tile = jobs[j - 2]["tile"]
                    dve.wait_ge(AM.pv_done, AM.first[j - 1])
                    nc.vector.tensor_copy(oT[:, tile, :], bank[6 + tile % 2][:, 0:S]).then_inc(AM.o_done, 1)
            q = 0
            for d2, br in enumerate(n["br"]):
                d = 2 * d2
                for i, (g, us) in enumerate(br):
                    dve.wait_ge(unit_done, us[-1] + 1)
                    dve.wait_ge(mix_s, 3 * d2 + i + 1)
                    gt = mix[:, 8 * i + d:8 * i + d + 2, :]
                    nc.vector.tensor_tensor(gt, gt, bank[g % 2][:, :].rearrange("p (a t) -> p a t", t=S), ALU.mult).then_inc(br_used, 1)
                dve.wait_ge(br_used, 3 * d2 + 3)
                g0, g1, g2 = (mix[:, 8 * i + d:8 * i + d + 2, :] for i in range(3))
                chain(dve, nc.vector.tensor_tensor(g0, g0, g1, ALU.add))
                nc.vector.tensor_tensor(g0, g0, g2, ALU.add).then_inc(mixed, 2)
            out_dve(dve, n)

        def bass_view(ap):
            got = []
            for g in range(B_G):
                a = ap[:, g, 0:S]
                got.append(bass.AP(tensor=a.tensor, offset=a.offset, ap=[list(a.ap[0]), [16, NCMP], [2, LC]]))
            return got

        def mixers_pe(pe, n):
            rms_pe(pe, n["ph"])

            def sums(q):
                pe.wait_ge(m_sq, q + 1)
                nc.tensor.matmul(bank[7][0:32, :], cst[:, C_E2 + 30 - 2 * q:C_E2 + 62 - 2 * q], msq[q % 2],
                                 start=(q == 0), stop=(q == NORMED - 1)).then_inc(m_ss, 1)

            pend = []
            q = 0
            for i, (kind, g, u) in enumerate(n["in"]):
                if kind == "nat":
                    proj_N(pe, g, u)
                else:
                    proj_T(pe, g, u, i == 0, n["ph"])
                while pend:
                    sums(pend.pop())
                if i in normed:
                    pend.append(q)
                    q += 1
                if 4 <= i < 8:
                    if i == 4:
                        pe.wait_ge(m_raw, 2)
                    for m in range(2 * (i - 4), 2 * (i - 3)):
                        tb, h = divmod(m, IDX_H)
                        wait(pe, i_r, m - 1)
                        half = h % 2
                        mm = nc.tensor.matmul(bank[2 + m % 2][:, 0:P * (tb + 1)], IQ[64 * half:64 * half + 64, h // 2, tb * P:(tb + 1) * P],
                                              IK[64 * half:64 * half + 64, 0:P * (tb + 1)], start=True, stop=True)
                        mm.then_inc(i_s, 1)
                if i == 8:
                    pe.wait_ge(cmpw_loaded, 48)
                    pe.wait_ge(k_blk, 2)
                    for l in range(LC):
                        mm = nc.tensor.matmul(bank[4][:, 0:30], cwk[:, l, :], cblk[0][:, l, :, :].rearrange("p g n -> p (g n)"),
                                              start=(l == 0), stop=(l == LC - 1))
                    mm.then_inc(k_mm, 1)
                    for l in range(LC):
                        mm = nc.tensor.matmul(bank[5][0:64, 0:30], cwv[:, l, :], cblk[1][:, l, :, :].rearrange("p g n -> p (g n)"),
                                              start=(l == 0), stop=(l == LC - 1))
                    mm.then_inc(k_mm, 1)
                if i == 10:
                    pe.wait_ge(k_c, 2)
                    nc.tensor.matmul(bank[4][:, 64:94], blk64, ksq, start=True, stop=True).then_inc(k_mm, 1)
                    pe.wait_ge(k_v, 1)
                    for g2 in range(B_G):
                        nc.tensor.transpose(bank[5][0:NCMP, 64 + 64 * g2:128 + 64 * g2], vcT[0:64, g2 * NCMP:(g2 + 1) * NCMP],
                                            ident[0:64, 0:64]).then_inc(k_mm, 1)
            while pend:
                sums(pend.pop())
            for q in range(NORMED):
                if q == 0:
                    pe.wait_ge(m_rr, 1)
                wait(pe, m_n, q - 1)
                nc.tensor.matmul(bank[2 + q % 2][:, :], cst[0:32, C_SEL + q * P:C_SEL + (q + 1) * P], rr[0:32, :],
                                 start=True, stop=True).then_inc(m_rb, 1)
            for j in range(NJ + 2):
                if j < NJ:
                    qk_pe(pe, AM, j)
                    for f in filler_at(j):
                        proj_T(pe, *n["mix"][f])
                if 1 <= j <= NJ:
                    tr_pe(pe, AM, j - 1)
                if j >= 2:
                    pv_pe(pe, AM, j - 2)
            pe.wait_ge(AM.o_done, 10)
            first = (6, 2, 0)
            for d2, br in enumerate(n["br"]):
                for i, (g, us) in enumerate(br):
                    b = take_bank(pe, g)
                    nk = (4, 4, 2)[i]
                    for a, u in enumerate(us):
                        wait_unit(pe, u)
                        w = slot(u, nk)
                        for k in range(nk):
                            mm = nc.tensor.matmul(b[:, a * S:(a + 1) * S], w[:, k, :], oT[:, first[i] + k, :],
                                                  start=(k == 0), stop=(k == nk - 1))
                        mm.then_inc(unit_done, 1)
            out_pe(pe, n, mix, KD, mixed)

        def ffn_act(act, n):
            rms_act(act, n["ph"])
            for i, (g, u) in enumerate(n["gu"]):
                act.wait_ge(unit_done, u + 1)
                wait(act, h_done, i - 1)
                nc.scalar.activation(sg[:, i % 2, :], bank[g % 2][:, 0:S], ACT.Silu).then_inc(h_silu, 1)

        def ffn_dve(dve, n):
            rms_dve(dve, n["ph"])
            for i, (g, u) in enumerate(n["gu"]):
                dve.wait_ge(h_silu, i + 1)
                nc.vector.tensor_tensor(zb[:, i, :], bank[g % 2][:, S:2 * S], sg[:, i % 2, :], ALU.mult).then_inc(h_done, 1)
            out_dve(dve, n)

        def ffn_pe(pe, n):
            rms_pe(pe, n["ph"])
            for i, (g, u) in enumerate(n["gu"]):
                proj_T(pe, g, u, i == 0, n["ph"])
            out_pe(pe, n, zb, KF, h_done)

        row_src = [("a_norm", 0, 0, 16), ("b_norm", 0, 16, 8), ("c_norm", 0, 24, 8), ("norm1_g_2", 0, 32, 8), ("norm2_g_2", 0, 40, 8)]

        SETUP_LOADS = 27
        block = ctx.enter_context(nc.Block())

        @block.sync
        def _(sp):
            n = [0]

            def load(dst, src):
                sp.dma_start(dst, src).then_inc(setup_loaded, 16)
                n[0] += 1

            load(xnat, t["x"][0].rearrange("(b p) d -> p b d", p=P))
            load(cst[:, :], t["cst"])
            for name, r, r0, nr in row_src:
                load(rows[r0:r0 + nr, r, :], t[name].rearrange("a (k p) -> (a k) p", p=P))
            load(rows[48:49, 0, :], t["b_q_norm"])
            load(rows[49:50, 0, :], t["b_k_norm"])
            for i in range(2):
                load(rows[50:56, 0, i * HD:(i + 1) * HD], t["qk_norm_g_2"][0])
            load(rows[56:88, 0, :], t["nsa_cmp_pos_2"][0].rearrange("w (l q) d -> (w l) (q d)", q=2))
            for i, name in enumerate(("a_conv_b", "a_ln_g", "a_ln_b")):
                load(rows[32 * i:32 * i + 32, 1, :], t[name].rearrange("a (k p) -> (a k) p", p=P))
            load(rows[0:48, 2, :], t["c_conv_w"][0].rearrange("a (k p) -> (a k) p", p=P))
            flat = t["a_conv_w"].rearrange("j a (k p) -> (j a k) p", p=P)
            for i in range(8):
                load(rows[0:124, 3 + i, :], flat[124 * i:124 * i + 124, :])
            load(hot, t["hot"])
            load(small[0:32, 224:224 + HEADS2], t["rel_bias_2"])
            load(fb, t["b_f_bias"].rearrange("a h -> h a"))
            assert n[0] == SETUP_LOADS
            for u, (_, parts) in enumerate(units):
                wait(sp, unit_done, u - RING + 1)
                for nk, at, width, src in parts:
                    sp.dma_start(slot(u, nk)[:, :, at:at + width], src).then_inc(unit_loaded[u % RING], 16)

        @block.gpsimd
        def _(pool):
            nc.gpsimd.memset(eps, EPS).then_inc(set_pool, 1)
            pool.wait_ge(set_pool, 1)
            nc.gpsimd.memset(small[32:33, 224:224 + HEADS2], 1.0).then_inc(set_pool, 1)
            pool.wait_ge(tab_copied, 4)
            for v, (h0, nh) in enumerate(((0, 16), (16, 4), (20, 4), (24, 4))):
                src = tabs[0:nh, v, :].unsqueeze(1).to_broadcast((nh, P, TABLE))
                pool.dma_start(skew[h0:h0 + nh, :, :], src).then_inc(skew_written, 16)
            pool.wait_ge(skew_written, 64)
            conf_pool(pool, conf0)
            conf_pool(pool, conf1)

        ROWS_OF = [88, 96, 48] + [124] * 8

        @block.tensor
        def _(pe):
            pe.wait_ge(setup_loaded, 16 * SETUP_LOADS)
            pe.wait_ge(set_pool, 2)
            for i in range(4):
                for a in range(2):
                    for tb in range(TB):
                        k = 2 * i + a
                        mm = nc.tensor.transpose(bank[i][:, a * S + tb * P:a * S + (tb + 1) * P], xnat[:, tb, k * P:(k + 1) * P], ident)
                mm.then_inc(set_done, 1)
            for i in range(11):
                if i >= 4:
                    pe.wait_ge(set_used, i - 3)
                nr = ROWS_OF[i]
                nc.tensor.transpose(bank[4 + i % 4][:, 0:nr], rows[0:nr, i, :], ident[0:nr, 0:nr]).then_inc(set_done, 1)
            for v, (h0, nh) in enumerate(((0, 16), (16, 4), (20, 4), (24, 4))):
                if v == 0:
                    pe.wait_ge(x_done, 4)
                nc.tensor.matmul(bank[v][0:nh, 0:TABLE], small[0:33, 224 + h0:224 + h0 + nh], hot[:, v * TABLE:(v + 1) * TABLE],
                                 start=True, stop=True).then_inc(tab_done, 1)
            pe.wait_ge(set_dve, 5)
            pe.wait_ge(tab_copied, 4)
            conf_pe(pe, conf0)
            fox_pe(pe, fox)
            short_pe(pe, short)
            conf_pe(pe, conf1)
            mixers_pe(pe, mixers)
            ffn_pe(pe, ffn)
            for i in range(4):
                pe.wait_ge(x_done, 4 * NPH + i + 1)
                for a in range(2):
                    for tb in range(TB):
                        k = 2 * i + a
                        mm = nc.tensor.transpose(bank[2 + i][:, a * S + tb * P:a * S + (tb + 1) * P], xT[:, k, tb * P:(tb + 1) * P], ident)
                mm.then_inc(set_done, 1)

        @block.vector
        def _(dve):
            for i in range(4):
                dve.wait_ge(set_done, i + 1)
                nc.vector.tensor_copy(xT[:, 2 * i:2 * i + 2, :], bank[i][:, :].rearrange("p (a t) -> p a t", t=S)).then_inc(x_done, 1)
            for i in range(11):
                dve.wait_ge(set_done, 5 + i)
                nr = ROWS_OF[i]
                if i < 3:
                    dst = cols[:, (0, 88, 184)[i]:(0, 88, 184)[i] + nr]
                else:
                    dst = convw[:, 124 * (i - 3):124 * (i - 2)]
                nc.vector.tensor_copy(dst, bank[4 + i % 4][:, 0:nr]).then_inc(set_used, 1)
            dve.wait_ge(set_used, 11)
            for i, (src, scale) in enumerate(((FQ, FD ** -0.5), (QK2, HD ** -0.5), (QK2 + 2, HD ** -0.5), (QK2 + 4, HD ** -0.5))):
                nc.vector.tensor_scalar(gq[:, i:i + 1], cols[:, src:src + 1], scale, None, ALU.mult).then_inc(set_dve, 1)
            nc.vector.memset(small[:, 6:7], 0.0).then_inc(set_dve, 1)
            for v, nh in enumerate((16, 4, 4, 4)):
                dve.wait_ge(tab_done, v + 1)
                nc.vector.tensor_copy(tabs[0:nh, v, :], bank[v][0:nh, 0:TABLE]).then_inc(tab_copied, 1)
            dve.wait_ge(skew_written, 64)
            conf_dve(dve, conf0)
            fox_dve(dve, fox)
            short_dve(dve, short)
            conf_dve(dve, conf1)
            mixers_dve(dve, mixers)
            ffn_dve(dve, ffn)
            for i in range(4):
                dve.wait_ge(set_done, 16 + i)
                src = bank[2 + i][:, :].rearrange("p (a b d) -> p b a d", a=2, b=TB)
                dst = xnat[:, :, 2 * i * P:(2 * i + 2) * P].rearrange("p b (a d) -> p b a d", a=2)
                for tb in range(TB):
                    nc.vector.tensor_copy(dst[:, tb, :, :], src[:, tb, :, :]).then_inc(set_dve, 1)

        @block.scalar
        def _(act):
            act.wait_ge(set_pool, 1)
            conf_act(act, conf0)
            fox_act(act, fox)
            short_act(act, short)
            conf_act(act, conf1)
            mixers_act(act, mixers)
            ffn_act(act, ffn)
            ov = out[0].rearrange("(b p) d -> p b d", p=P)
            for i in range(4):
                act.wait_ge(set_dve, 5 + 2 * i + 2)
                act.dma_start(ov[:, :, 2 * i * P:(2 * i + 2) * P], xnat[:, :, 2 * i * P:(2 * i + 2) * P]).then_inc(out_stored, 16)
            act.wait_ge(out_stored, 64)


_INS = ["x", "a_norm", "a_w_in", "a_conv_w", "a_conv_b", "a_ln_g", "a_ln_b", "a_w_out", "b_norm", "b_w_in", "b_f_bias",
        "b_q_norm", "b_k_norm", "b_w_out", "c_norm", "c_w_in", "c_conv_w", "c_w_out", "norm1_g_2", "norm2_g_2",
        "w_in_2", "qk_norm_g_2", "nsa_cmp_pos_2", "nsa_cmp_w_2", "w_branch_a_2", "w_branch_b_2", "w_branch_c_2",
        "w_out_2", "w_ffn_in_2", "w_ffn_out_2", "rel_bias_2"]


def kernel(**inputs):
    import numpy as _np
    import concourse.bacc as _bacc
    from concourse import mybir as _mybir
    from concourse.bass_utils import run_bass_kernel_spmd as _run

    nc = _bacc.Bacc("TRN2", target_bir_lowering=False, num_devices=1)
    arrays, args = {}, {}
    cst, hot = constants()
    given = [(name, _np.ascontiguousarray(inputs[name])) for name in _INS] + [("cst", cst), ("hot", hot)]
    for name, a in given:
        arrays[f"in_{name}_dram"] = a
        args[name] = nc.dram_tensor(f"in_{name}_dram", a.shape, _mybir.dt.from_np(a.dtype), kind="ExternalInput").ap()
    out = nc.dram_tensor("out_0_dram", (1, S, D), F32, kind="ExternalOutput").ap()
    program(nc, args, out)
    r = _run(nc, [arrays], core_ids=[0])
    return r.results[0]["out_0_dram"]
```

```python
from contextlib import ExitStack

import numpy as np

import concourse.bass as bass
from concourse import mybir

F32 = mybir.dt.float32
F32R = mybir.dt.float32r
ALU = mybir.AluOpType
ACT = mybir.ActivationFunctionType
AX = mybir.AxisListType.X

P = 128
S = 256
TB = S // P
D = 1024
KD = D // P
E = 2048
KE = E // P
NEG = -1e30
EPS = 1e-6
TAPS = 31
TAPS_DVE = 20
TAPS_POOL = TAPS - TAPS_DVE
SHORT = 3
FH = 16
FD = E // FH
HD = 64
TOPK = 64
A_H, IDX_H, B_H, B_G, C_H, C_SLOTS, C_GROUPS = 8, 4, 8, 2, 12, 4, ((128, 1), (512, 4), (2048, 16))
NCMP = (S - 32) // 16 + 1
LC = 16
FF = 2816
KF = FF // P
OFF_AK, OFF_AV, OFF_IQ, OFF_IK, OFF_IW, OFF_BQ = 512, 576, 640, 896, 960, 964
OFF_KV, OFF_BG, OFF_CQ, OFF_CK, OFF_CV, OFF_MIX = 1476, 2244, 2268, 3036, 3804, 4572
RING = 3
HALVES = 4
HALF = KD * P
UNIT = KD * 2 * P
TABLE = 384
HEADS2 = A_H + B_H + C_H

C_ID, C_ONE, C_B64, C_E1, C_E2 = 0, 128, 256, 384, 384 + 31
C_MASK = C_E2 + 62
C_CMP = C_MASK + S
C_END = C_CMP + 2 * NCMP
NORMED = 13


def rel_bucket(dist):
    n = np.maximum(dist, 0)
    nf = np.maximum(n, 1).astype(np.float32)
    large = 16 + (np.log(nf / np.float32(16)) / np.float32(np.log(2048 / 16)) * np.float32(16)).astype(np.int32)
    return np.where(n < 16, n, np.minimum(large, 31))


def constants():
    c = np.zeros((P, C_END), np.float32)
    p = np.arange(P)
    c[:, C_ID:C_ID + P] = np.eye(P)
    c[:, C_ONE:C_ONE + P] = 1.0
    c[:, C_B64:C_B64 + P] = (p[:, None] // 64) == (p[None, :] // 64)
    c[:, C_E1 + 15] = 1.0
    c[:64, C_E2 + 30] = 1.0
    c[64:, C_E2 + 31] = 1.0
    c[:, C_MASK:C_MASK + S] = np.where(P + p[:, None] - np.arange(S)[None, :] >= 0, 0.0, NEG)
    for tb in range(TB):
        end = 16 * np.arange(NCMP)[None, :] + 31
        c[:, C_CMP + tb * NCMP:C_CMP + (tb + 1) * NCMP] = np.where(end <= tb * P + p[:, None], 0.0, NEG)
    sel = np.zeros((32, NORMED * P), np.float32)
    for g in range(NORMED):
        for half in range(2):
            sel[2 * g + half, g * P + 64 * half:g * P + 64 * half + 64] = 1.0
    hot = np.zeros((33, 4, TABLE), np.float32)
    dist = S - 1 - np.arange(TABLE)
    for v in range(4):
        ok = dist >= 0
        if v:
            window, step = C_GROUPS[v - 1]
            ok &= (dist <= window) & (dist % step == 0)
        hot[rel_bucket(dist)[ok], v, np.nonzero(ok)[0]] = 1.0
        hot[32, v, ~ok] = NEG
    return c, hot.reshape(33, 4 * TABLE), sel


def program(nc, t, out):
    ctx = ExitStack()
    with ctx:
        place = [(nc.sbuf_base + 31) // 32 * 32]

        def sb(name, cols, rows=P, dt=F32):
            at = place[0]
            place[0] += (4 * cols + 31) // 32 * 32
            return nc.alloc_sbuf_tensor_at(name, [rows, cols], dt, offset=at)

        def over(name, at, tiles):
            return nc.alloc_sbuf_tensor_at(name, [P, tiles * S], F32R, offset=at)[:, :].rearrange("p (k t) -> p k t", t=S)

        def sem(name):
            return ctx.enter_context(nc.semaphore(name))

        cst = sb("cst", C_END)
        ident = cst[:, C_ID:C_ID + P]
        ones = cst[:, C_ONE:C_ONE + P]
        blk64 = cst[:, C_B64:C_B64 + P]
        xT = sb("xT", KD * S)[:, :].rearrange("p (k t) -> p k t", t=S)
        sqb = sb("sqb", KD * S)[:, :].rearrange("p (k t) -> p k t", t=S)
        xh = sb("xh", KD * S, dt=F32R)[:, :].rearrange("p (k t) -> p k t", t=S)
        xl = sb("xl", KD * S, dt=F32R)[:, :].rearrange("p (k t) -> p k t", t=S)
        std = sb("std", 2 * S)
        rr = sb("rr", 2 * S)
        ring = sb("ring", RING * UNIT)
        whi = sb("whi", HALVES * HALF, dt=F32R)
        wlo = sb("wlo", HALVES * HALF, dt=F32R)
        at_wide = place[0]
        wide = sb("wide", 38 * S)
        yb = wide[:, 0:KE * S].rearrange("p (k t) -> p k t", t=S)
        zb = wide[:, KE * S:38 * S].rearrange("p (k t) -> p k t", t=S)
        T = wide[:, 0:HEADS2 * S].rearrange("p (h s) -> p h s", s=S)
        oT = wide[:, HEADS2 * S:38 * S].rearrange("p (k t) -> p k t", t=S)
        at_qk = place[0]
        qk = sb("qk", 16 * 2 * S)[:, :].rearrange("p (g a t) -> p g a t", a=2, t=S)
        qk_tiles = qk.rearrange("p g a t -> p (g a) t")
        at_vb = place[0]
        vb_flat = sb("vb", TB * E)
        vb = vb_flat[:, :].rearrange("p (b n) -> p b n", b=TB)
        y_hi = over("y_hi", at_wide, KE)
        y_lo = over("y_lo", at_wide + 4 * KE * S, KF)
        h_lo = over("h_lo", at_qk, KF)
        m_hl = over("m_hl", at_vb, 2 * KD)

        def mixt(i):
            return wide[:, (16 + i) * S:(18 + i) * S].rearrange("p (k t) -> p k t", t=S) if i < 12 else qk_tiles[:, 4 + i:6 + i, :]

        cols = sb("cols", 88 + 96 + 48)
        convw = sb("convw", 2 * TAPS * KE)
        taps = convw[:, :].rearrange("p (j k c) -> p j k c", j=2, k=TAPS)
        small = sb("small", 256)
        scratch = sb("scratch", 4608)
        qk_flat = qk[:, :, :, :].rearrange("p g a t -> p (g a t)")
        rows = qk_flat[:, 0:11 * P].rearrange("p (r c) -> p r c", c=P)
        hot = qk_flat[0:33, 11 * P:11 * P + 4 * TABLE]
        tabs = qk_flat[0:16, 11 * P + 4 * TABLE:11 * P + 8 * TABLE].rearrange("p (v j) -> p v j", j=TABLE)
        xnat = yb[:, 0:8, :].rearrange("p k t -> p (k t)").rearrange("p (b d) -> p b d", b=TB)
        UPW = TAPS - 1 + S
        up = scratch[:, 0:3 * UPW].rearrange("p (r w) -> p r w", w=UPW)
        tmp = scratch[:, 900:900 + 4 * S].rearrange("p (r w) -> p r w", w=S)
        accp = scratch[:, 1924:1924 + 2 * S].rearrange("p (r w) -> p r w", w=S)
        acca = scratch[:, 2436:2436 + 2 * S].rearrange("p (r w) -> p r w", w=S)
        sg = scratch[:, 2948:2948 + 2 * S].rearrange("p (r w) -> p r w", w=S)
        sq4 = scratch[:, 3460:3460 + 4 * S].rearrange("p (r w) -> p r w", w=S)
        Lb = scratch[:, 0:6 * 384].rearrange("p (r w) -> p r w", w=384)
        PT = scratch[:, 2304:2304 + 6 * 384].rearrange("p (r w) -> p r w", w=384)
        bank = [ctx.enter_context(nc.psum_tensor(f"bank{i}", [P, 512], F32)) for i in range(8)]
        skew = nc.dram_tensor("skew", (HEADS2, P, TABLE), F32, kind="Internal").ap()

        def norm_g(i, k):
            return cols[:, 8 * i + k:8 * i + k + 1]
        FQ, FK, QK2, POS, ROWB, ROWC = 48, 49, 50, 56, 88, 88 + 96
        def short_w(k, c):
            return cols[:, ROWC + k * KE + c:ROWC + k * KE + c + 1]
        eps = small[:, 0:1]
        gq = small[:, 1:6]
        fb = small[0:FH, 8:9]
        gate_s = small[:, 16:16 + TB * 24].rearrange("p (b n) -> p b n", b=TB)
        mstat = small[:, 64:64 + 18].rearrange("p (r n) -> p r n", r=3)
        nstat = small[:, 84:84 + 18].rearrange("p (r n) -> p r n", r=3)
        sstat = small[:, 104:104 + 18].rearrange("p (r n) -> p r n", r=3)
        fstat = small[:, 124:124 + 18].rearrange("p (r n) -> p r n", r=3)
        jstat = small[:, 144:144 + 12].rearrange("p (r n) -> p r n", r=3)
        best = small[:, 160:160 + 2 * 8].rearrange("p (r n) -> p r n", r=2)

        setup_loaded = sem("setup_loaded")
        unit_loaded = [sem(f"unit_loaded{i}") for i in range(RING)]
        half_done = sem("half_done")
        hi_done = sem("hi_done")
        lo_dve = sem("lo_dve")
        lo_pool = sem("lo_pool")
        y_raw = sem("y_raw")
        y_hid = sem("y_hid")
        y_split = sem("y_split")
        xr_done = sem("xr_done")
        xh_done = sem("xh_done")
        sel_loaded = sem("sel_loaded")
        set_done = sem("set_done")
        set_used = sem("set_used")
        set_pool = sem("set_pool")
        set_dve = sem("set_dve")
        tab_done = sem("tab_done")
        tab_copied = sem("tab_copied")
        skew_written = sem("skew_written")
        T_loaded = sem("T_loaded")
        cmpw_loaded = sem("cmpw_loaded")
        x_done = sem("x_done")
        sq_done = sem("sq_done")
        ss_done = sem("ss_done")
        std_done = sem("std_done")
        rr_done = sem("rr_done")
        xn_done = sem("xn_done")
        step = sem("dve_step")
        out_stored = sem("out_stored")
        steps = [0]

        def wait(eng, s, value):
            if value > 0:
                eng.wait_ge(s, value)

        def chain(dve, ins):
            steps[0] += 1
            ins.then_inc(step, 1)
            dve.wait_ge(step, steps[0])

        units = []

        def unit_in(w, segments, dve=False, plain=False):
            parts, at = [], 0
            for c0, n in segments:
                parts.append((KD, at, n, w[:, c0:c0 + n].rearrange("(k p) n -> p k n", p=P)))
                at += n
            units.append((at, parts))
            cut(len(units) - 1, True, dve, plain)
            return len(units) - 1

        def unit_out(w, k0, nk, d, dve=True):
            src = w[k0 * P:(k0 + nk) * P, d * P:(d + 1) * P].rearrange("(k p) n -> p k n", p=P)
            units.append((P, [(nk, 0, P, src)]))
            cut(len(units) - 1, False, dve)
            return len(units) - 1

        def raw(u, nk):
            w = units[u][0]
            at = (u % RING) * UNIT
            return ring[:, at:at + nk * w].rearrange("p (k n) -> p k n", n=w)

        halves = []
        splits = []
        n_hi = []
        first_half = []

        def cut(u, by_columns, dve, plain=False):
            first_half.append(len(halves))
            w, nk = units[u][0], units[u][1][0][0]
            src = raw(u, nk)
            if by_columns:
                pieces = [(src[:, :, c:min(c + P, w)], nk, min(P, w - c)) for c in range(0, w, P)]
            else:
                per = -(-nk // -(-nk // KD))
                pieces = [(src[:, k:min(k + per, nk), :], min(per, nk - k), w) for k in range(0, nk, per)]
            for i, (ap, k, n) in enumerate(pieces):
                halves.append((u, ap, k, n, dve and len(halves) % 2 == 0))
                if not plain:
                    splits.append(len(halves) - 1)
                n_hi.append(len(splits))

        def hs(u):
            return range(first_half[u], first_half[u + 1] if u + 1 < len(first_half) else len(halves))

        def last(u):
            return hs(u)[-1]

        def is_split(h):
            return n_hi[h] > (n_hi[h - 1] if h else 0)

        def ahead(u):
            q = n_hi[last(u)] - is_split(last(u)) + HALVES - 1
            plain = [v for v in range(u, len(units)) if not is_split(last(v))][:1]
            hs_ = [h for h in splits[:q + 1] if not plain or halves[h][0] < plain[0] + RING]
            return hs_[-1] if hs_ else -1

        def piece(buf, h):
            _, _, k, n, _ = halves[h]
            n = P if n == FH else n
            at = ((n_hi[h] - 1) % HALVES) * HALF
            return buf[:, at:at + k * n].rearrange("p (k n) -> p k n", n=n)

        def landed(eng, u):
            before = sum(len(units[v][1]) for v in range(u % RING, u + 1, RING))
            eng.wait_ge(unit_loaded[u % RING], 16 * before)

        def n_dve(h):
            return sum(halves[i][4] for i in splits[:n_hi[h]])

        def split_ready(pe, h):
            pe.wait_ge(hi_done, n_hi[h])
            if halves[h][4]:
                pe.wait_ge(lo_dve, n_dve(h))
            else:
                pe.wait_ge(lo_pool, n_hi[h] - n_dve(h))

        hi_at, dve_at, pool_at = [0], [0], [0]

        def hi_to(act, h_last):
            while hi_at[0] <= min(h_last, len(halves) - 1):
                h = hi_at[0]
                hi_at[0] += 1
                if not is_split(h):
                    continue
                u, src, k, n, _ = halves[h]
                landed(act, u)
                q = n_hi[h] - 1
                if q >= HALVES:
                    act.wait_ge(half_done, splits[q - HALVES] + 1)
                nc.scalar.copy(piece(whi, h)[:, :, 0:n], src).then_inc(hi_done, 1)

        def lo_to(eng, engine, at, mine, done, h_last):
            while at[0] <= min(h_last, len(halves) - 1):
                h = at[0]
                u, src, k, n, dve = halves[h]
                if is_split(h) and dve == mine:
                    eng.wait_ge(hi_done, n_hi[h])
                    engine.tensor_tensor(piece(wlo, h)[:, :, 0:n], src, piece(whi, h)[:, :, 0:n].bitcast(F32),
                                         ALU.subtract).then_inc(done, 1)
                at[0] += 1

        def lo_dve_to(dve, h_last):
            lo_to(dve, nc.vector, dve_at, True, lo_dve, h_last)

        def lo_pool_to(pool, h_last):
            lo_to(pool, nc.gpsimd, pool_at, False, lo_pool, h_last)

        groups = []

        def group(free):
            groups.append(free)
            return len(groups) - 1

        def take_bank(pe, g):
            if g >= 2:
                wait(pe, *groups[g - 2])
            return bank[g % 2]

        NPH = 6
        def x_free(ph, g):
            return (x_done, 4 * ph + 4 + g + 1)

        def plan_out(ph, w, nk, per):
            got = []
            for g in range(4):
                us = [unit_out(w, k0, per, 2 * g + a) for a in range(2) for k0 in range(0, nk, per)]
                got.append((group(x_free(ph, g)), us))
            return got

        u_done, sg_done, sz_done = sem("u_done"), sem("sg_done"), sem("sz_done")
        tmp_done, tap_done, conv_done = sem("tmp_done"), sem("tap_done"), sem("conv_done")
        mean_done, dc_done, sqd_done, sqm_done = sem("mean_done"), sem("dc_done"), sem("sqd_done"), sem("sqm_done")
        lstd_done, dn_done, act_done = sem("lstd_done"), sem("dn_done"), sem("act_done")
        pad_done = sem("pad_done")

        def plan_conf(ph, j):
            w = t["a_w_in"][j]
            n = {"ph": ph, "j": j}
            n["vg"], n["z"] = [], []

            def z_group(i):
                n["z"].append((group((sz_done, j * 8 + i + 1)), unit_in(w, [(2 * E + i * 2 * P, 2 * P)], True)))

            for c in range(KE):
                n["vg"].append((group((u_done, j * KE + c + 1)), unit_in(w, [(c * P, P), (E + c * P, P)], plain=True)))
                if c % 4 == 3:
                    z_group(c // 4)
            for i in range(4, 8):
                z_group(i)
            n["out"] = plan_out(ph, t["a_w_out"][j], KE, KE)
            return n

        f_raw, f_sq, f_ss, f_std, f_rr = sem("f_raw"), sem("f_sq"), sem("f_ss"), sem("f_std"), sem("f_rr")
        f_rb, f_n, f_c, f_v, f_z, f_e = sem("f_rb"), sem("f_n"), sem("f_c"), sem("f_v"), sem("f_z"), sem("f_e")

        def plan_fox(ph):
            w = t["b_w_in"][0]
            n = {"ph": ph}
            n["f"] = (group((f_e, 1)), unit_in(w, [(4 * E, FH)], True))
            n["qk"] = [(group((f_raw, h + 1)), unit_in(w, [(h * P, P), (E + h * P, P)], True)) for h in range(FH)]
            n["z"], n["v"], n["at"] = [], [], {}
            for j in range(-3, FH):
                if j < 0 or (j >= 3 and j % 2 == 1 and len(n["z"]) < 8):
                    i = len(n["z"])
                    n["z"].append((group((f_z, i + 1)), unit_in(w, [(3 * E + i * 2 * P, 2 * P)], True)))
                    n["at"][j] = ("z", i)
                elif j % 2 == 0:
                    i = len(n["v"])
                    n["v"].append((group((f_v, i + 1)), unit_in(w, [(2 * E + i * 2 * P, 2 * P)], plain=True)))
                    n["at"][j] = ("v", i)
            assert len(n["z"]) == len(n["v"]) == 8
            n["out"] = plan_out(ph, t["b_w_out"][0], KE, KE)
            return n

        c_cg, c_cu, c_sz = sem("c_cg"), sem("c_cu"), sem("c_sz")

        def plan_short(ph):
            w = t["c_w_in"][0]
            n = {"ph": ph, "uc": [], "bz": []}
            for c in range(KE):
                n["uc"].append((group((c_cu, c + 1)), unit_in(w, [(c * P, P), (2 * E + c * P, P)], True)))
                n["bz"].append((group((y_raw, 32 + c + 1)), unit_in(w, [(E + c * P, P), (3 * E + c * P, P)], True)))
            n["out"] = plan_out(ph, t["c_w_out"][0], KE, KE)
            return n

        m_raw, m_sq, m_ss, m_std, m_rr = sem("m_raw"), sem("m_sq"), sem("m_ss"), sem("m_std"), sem("m_rr")
        m_rb, m_n, m_mix = sem("m_rb"), sem("m_n"), sem("m_mix")

        br_used, mix_s, mixed = sem("br_used"), sem("mix_s"), sem("mixed")
        oh_done, ol_done, mh_done, ml_done = sem("oh_done"), sem("ol_done"), sem("mh_done"), sem("ml_done")

        def plan_mixers(ph):
            w = t["w_in_2"][0]
            kv = [OFF_KV + 128 * i for i in range(6)]
            def dup2(c0):
                return [(c0, HD), (c0, HD), (c0 + HD, HD), (c0 + HD, HD)]
            order = [("raw", [(OFF_AK, HD), (OFF_AK, HD), (OFF_IK, HD), (OFF_IK, HD)]),
                     ("raw", [(OFF_IQ, 2 * P)]),
                     ("nat", [(OFF_AV, HD), (kv[3], P), (OFF_IW, IDX_H), (OFF_BG, 3 * B_H)]),
                     ("cmp", dup2(kv[0])), ("cmp", dup2(kv[1]))]
            order += [("raw", [(i * 2 * P, 2 * P)]) for i in range(2)]
            order += [("raw", [(OFF_BQ + i * 2 * P, 2 * P)]) for i in range(2)]
            order += [("raw", dup2(kv[2])), ("raw", dup2(kv[4]))]
            order += [("raw", [(OFF_CQ + i * 2 * P, 2 * P)]) for i in range(3)]
            order += [("raw", [(OFF_CK + i * 2 * P, 2 * P)]) for i in range(3)]
            order += [("nat", [(kv[5], P)])] + [("nat", [(OFF_CV + i * 2 * P, 2 * P)]) for i in range(3)]
            n = {"ph": ph, "in": []}
            for i, (kind, segments) in enumerate(order):
                n["in"].append((kind, group((m_raw, i + 1)), unit_in(w, segments, plain=(kind == "nat"))))
            n["mix"] = [(group((m_mix, i + 1)), unit_in(w, [(OFF_MIX + i * 2 * P, 2 * P)], True)) for i in range(12)]
            n["br"] = []
            for d in range(0, KD, 2):
                ua = [unit_out(t["w_branch_a_2"][0], 0, 4, d + a) for a in range(2)]
                ub = [unit_out(t["w_branch_b_2"][0], 0, 4, d + a) for a in range(2)]
                uc = [unit_out(t["w_branch_c_2"][0], 0, 2, d + a) for a in range(2)]
                gs = [group((br_used, 3 * (d // 2) + i + 1)) for i in range(3)]
                n["br"].append(list(zip(gs, (ua, ub, uc))))
            n["out"] = plan_out(ph, t["w_out_2"][0], KD, KD)
            return n

        h_silu = sem("h_silu")

        def plan_ffn(ph):
            w = t["w_ffn_in_2"][0]
            n = {"ph": ph}
            n["gu"] = [(group((y_raw, 64 + i + 1)), unit_in(w, [(i * P, P), (FF + i * P, P)], True)) for i in range(KF)]
            n["out"] = plan_out(ph, t["w_ffn_out_2"][0], KF, KF // 2)
            return n

        conf0 = plan_conf(0, 0)
        fox = plan_fox(1)
        short = plan_short(2)
        conf1 = plan_conf(3, 1)
        mixers = plan_mixers(4)
        ffn = plan_ffn(5)
        GAIN = [0, 2, 3, 1, 4, 5]

        def rms_act(act, ph):
            for g in range(4):
                act.wait_ge(x_done, 4 * ph + g + 1)
                nc.scalar.activation(sqb[:, 2 * g:2 * g + 2, :], xT[:, 2 * g:2 * g + 2, :], ACT.Square).then_inc(sq_done, 1)
            act.wait_ge(ss_done, ph + 1)
            nc.scalar.activation(std[:, 0:S], bank[7][:, 0:S], ACT.Sqrt, scale=1.0 / D, bias=eps).then_inc(std_done, 1)
            for g in range(4):
                act.wait_ge(xr_done, KD * ph + 2 * g + 2)
                nc.scalar.copy(xh[:, 2 * g:2 * g + 2, :], sqb[:, 2 * g:2 * g + 2, :]).then_inc(xh_done, 1)

        def rms_pe(pe, ph):
            for k in range(KD):
                pe.wait_ge(sq_done, 4 * ph + k // 2 + 1)
                mm = nc.tensor.matmul(bank[7][:, 0:S], ones, sqb[:, k, :], start=(k == 0), stop=(k == KD - 1))
            mm.then_inc(ss_done, 1)

        def rms_dve(dve, ph):
            dve.wait_ge(std_done, ph + 1)
            nc.vector.reciprocal(rr[:, 0:S], std[:, 0:S]).then_inc(rr_done, 1)
            dve.wait_ge(rr_done, ph + 1)
            def low(g):
                dve.wait_ge(xh_done, 4 * ph + g + 1)
                nc.vector.tensor_tensor(xl[:, 2 * g:2 * g + 2, :], sqb[:, 2 * g:2 * g + 2, :],
                                        xh[:, 2 * g:2 * g + 2, :].bitcast(F32), ALU.subtract).then_inc(xn_done, 1)

            for k in range(KD):
                nc.vector.scalar_tensor_tensor(sqb[:, k, :], xT[:, k, :], norm_g(GAIN[ph], k), rr[:, 0:S],
                                               ALU.mult, ALU.mult).then_inc(xr_done, 1)
                if k % 2 == 1 and k >= 3:
                    low(k // 2 - 1)
            low(3)

        def products(out, pairs):
            n = len(pairs)
            for i, ((lh, ll), (rh, rl)) in enumerate(pairs):
                nc.tensor.matmul(out, lh, rh, start=(i == 0), stop=False)
                nc.tensor.matmul(out, lh, rl, start=False, stop=False)
                mm = nc.tensor.matmul(out, ll, rh, start=False, stop=(i == n - 1))
            return mm

        def proj_T(pe, g, u, first=False, ph=0):
            b = take_bank(pe, g)
            for a, h in enumerate(hs(u)):
                o = b[:, a * S:(a + 1) * S]
                if is_split(h):
                    split_ready(pe, h)
                    wh, wl = piece(whi, h), piece(wlo, h)
                else:
                    landed(pe, u)
                for k in range(KD):
                    if first and a == 0:
                        pe.wait_ge(xn_done, 4 * ph + k // 2 + 1)
                    if not is_split(h):
                        mm = nc.tensor.matmul(o, halves[h][1][:, k, :], sqb[:, k, :], start=(k == 0), stop=(k == KD - 1))
                        continue
                    nc.tensor.matmul(o, wh[:, k, :], xh[:, k, :], start=(k == 0), stop=False)
                    nc.tensor.matmul(o, wh[:, k, :], xl[:, k, :], start=False, stop=False)
                    mm = nc.tensor.matmul(o, wl[:, k, :], xh[:, k, :], start=False, stop=(k == KD - 1))
                mm.then_inc(half_done, 1)

        def proj_N(pe, g, u):
            b = take_bank(pe, g)
            landed(pe, u)
            w = units[u][0]
            for tb in range(TB):
                for k in range(KD):
                    mm = nc.tensor.matmul(b[:, tb * S:tb * S + w], sqb[:, k, tb * P:(tb + 1) * P], raw(u, KD)[:, k, :],
                                          start=(k == 0), stop=(k == KD - 1))
            mm.then_inc(half_done, len(hs(u)))

        def out_pe(pe, n, hi, lo, nk, ready, base=0):
            seen = set()
            for g, us in n["out"]:
                b = take_bank(pe, g)
                hh = [h for u in us for h in hs(u)]
                k0 = 0
                for h in hh:
                    split_ready(pe, h)
                    wh, wl = piece(whi, h), piece(wlo, h)
                    a, kk = divmod(k0, nk)
                    o = b[:, a * S:(a + 1) * S]
                    for k in range(halves[h][2]):
                        if kk + k not in seen:
                            seen.add(kk + k)
                            pe.wait_ge(ready, base + kk + k + 1)
                        nc.tensor.matmul(o, wh[:, k, :], hi[:, kk + k, :], start=(kk + k == 0), stop=False)
                        nc.tensor.matmul(o, wh[:, k, :], lo[:, kk + k, :], start=False, stop=False)
                        mm = nc.tensor.matmul(o, wl[:, k, :], hi[:, kk + k, :], start=False, stop=(kk + k == nk - 1))
                    k0 += halves[h][2]
                    mm.then_inc(half_done, 1)

        def group_done(eng, u):
            eng.wait_ge(half_done, last(u) + 1)

        def act_ahead(act, u):
            hi_to(act, ahead(u))

        def dve_ahead(dve, u):
            lo_dve_to(dve, ahead(u))

        def out_act(act, n):
            for g, us in n["out"]:
                act_ahead(act, us[-1])

        def out_dve(dve, n):
            for i, (g, us) in enumerate(n["out"]):
                dve_ahead(dve, us[-1])
                group_done(dve, us[-1])
                nc.vector.tensor_tensor(xT[:, 2 * i:2 * i + 2, :], bank[g % 2][:, :].rearrange("p (a t) -> p a t", t=S),
                                        xT[:, 2 * i:2 * i + 2, :], ALU.add).then_inc(x_done, 1)

        yr = sb("yr", 3 * S)[:, :].rearrange("p (r t) -> p r t", t=S)

        def y_slot(eng, m):
            wait(eng, y_split, m - 2)
            return yr[:, m % 3, :]

        def y_high(act, m, dst):
            act.wait_ge(y_raw, m + 1)
            nc.scalar.copy(dst, yr[:, m % 3, :]).then_inc(y_hid, 1)

        def y_low(dve, m, hi, dst):
            dve.wait_ge(y_hid, m + 1)
            nc.vector.tensor_tensor(dst, yr[:, m % 3, :], hi.bitcast(F32), ALU.subtract).then_inc(y_split, 1)

        for n_, y0 in ((conf0, 0), (fox, 16), (short, 32), (conf1, 48), (ffn, 64)):
            n_["y0"] = y0

        Z_BESIDE = {1: 5, 4: 6, 8: 7}

        def conf_z(act, n, i):
            g, u = n["z"][i]
            act_ahead(act, u)
            group_done(act, u)
            nc.scalar.activation(zb[:, 2 * i:2 * i + 2, :], bank[g % 2][:, :].rearrange("p (a t) -> p a t", t=S),
                                 ACT.Silu).then_inc(sz_done, 1)

        def conf_act(act, n):
            j = n["j"]
            rms_act(act, n["ph"])

            def sigmoid(c):
                if c % 4 == 0 and c:
                    conf_z(act, n, c // 4 - 1)
                g, u = n["vg"][c]
                act_ahead(act, u)
                group_done(act, u)
                if c >= 2:
                    act.wait_ge(u_done, j * KE + c - 1)
                nc.scalar.activation(sg[:, c % 2, :], bank[g % 2][:, S:2 * S], ACT.Sigmoid).then_inc(sg_done, 1)

            sigmoid(0)
            for c in range(KE):
                act.wait_ge(u_done, j * KE + c + 1)
                for i in range(TAPS_POOL):
                    if i == TAPS_POOL // 3 and c + 1 < KE:
                        sigmoid(c + 1)
                    k = TAPS_DVE + i
                    m = (j * KE + c) * TAPS_POOL + i
                    wait(act, tap_done, m - 3)
                    src = up[:, c % 3, k:k + S]
                    bias = cols[:, ROWB + j * KE + c:ROWB + j * KE + c + 1] if i == 0 else 0.0
                    nc.scalar.activation(tmp[:, m % 4, :], src, ACT.Identity, scale=taps[:, j, k, c:c + 1],
                                         bias=bias).then_inc(tmp_done, 1)
            conf_z(act, n, 3)
            conf_z(act, n, 4)
            for c in range(KE):
                act.wait_ge(dc_done, j * KE + c + 1)
                if c >= 4:
                    act.wait_ge(sqm_done, j * KE + c - 3)
                nc.scalar.activation(sq4[:, c % 4, :], yb[:, c, :], ACT.Square).then_inc(sqd_done, 1)
            act.wait_ge(sqm_done, j * KE + KE)
            nc.scalar.activation(std[:, 0:S], bank[6][:, 0:S], ACT.Sqrt, scale=1.0 / E, bias=eps).then_inc(lstd_done, 1)
            for c in range(KE + 2):
                if c >= 2:
                    y_high(act, n["y0"] + c - 2, y_hi[:, c - 2, :])
                if c >= KE:
                    continue
                if c in Z_BESIDE:
                    conf_z(act, n, Z_BESIDE[c])
                act.wait_ge(dn_done, j * KE + c + 1)
                lg = cols[:, ROWB + 32 + j * KE + c:ROWB + 32 + j * KE + c + 1]
                lb = cols[:, ROWB + 64 + j * KE + c:ROWB + 64 + j * KE + c + 1]
                nc.scalar.activation(yb[:, c, :], yb[:, c, :], ACT.Silu, scale=lg, bias=lb).then_inc(act_done, 1)
            out_act(act, n)

        def write_skew(pool):
            pool.wait_ge(tab_copied, 4)
            for v, (h0, nh) in enumerate(((0, 16), (16, 4), (20, 4), (24, 4))):
                src = tabs[0:nh, v, :].unsqueeze(1).to_broadcast((nh, P, TABLE))
                pool.dma_start(skew[h0:h0 + nh, :, :], src).then_inc(skew_written, 16)

        def conf_pool(pool, n):
            j = n["j"]
            for c in range(KE):
                if j == 0 and c == 2:
                    write_skew(pool)
                for i in range(1, TAPS_POOL):
                    if i == TAPS_POOL // 2 and c + 1 < KE:
                        lo_pool_to(pool, ahead(n["vg"][c + 1][1]))
                    m = (j * KE + c) * TAPS_POOL + i
                    pool.wait_ge(tmp_done, m + 1)
                    if i == 1 and c >= 2:
                        pool.wait_ge(conv_done, j * KE + c - 1)
                    a = tmp[:, (m - 1) % 4, :] if i == 1 else accp[:, c % 2, :]
                    if i > 1:
                        pool.wait_ge(tap_done, m)
                    nc.gpsimd.tensor_tensor(accp[:, c % 2, :], a, tmp[:, m % 4, :], ALU.add)\
                        .then_inc(tap_done, 2 if i == 1 else 1)
            lo_pool_to(pool, ahead(n["z"][4][1]))
            for c in range(KE):
                if c in Z_BESIDE:
                    lo_pool_to(pool, ahead(n["z"][Z_BESIDE[c]][1]))
                pool.wait_ge(act_done, j * KE + c + 1)
                wait(pool, sz_done, j * 8 + c // 2 + 1)
                nc.gpsimd.tensor_tensor(y_slot(pool, n["y0"] + c), yb[:, c, :], zb[:, c, :], ALU.mult).then_inc(y_raw, 1)
            lo_pool_to(pool, last(n["out"][-1][1][-1]))

        def conf_dve(dve, n):
            j = n["j"]
            for r in range(3):
                nc.vector.memset(up[:, r, 0:TAPS - 1], 0.0).then_inc(pad_done, 1)
            dve.wait_ge(pad_done, 3 * j + 3)
            rms_dve(dve, n["ph"])

            def gated(c):
                g, u = n["vg"][c]
                dve.wait_ge(sg_done, j * KE + c + 1)
                if c >= 3:
                    wait(dve, tmp_done, (j * KE + c - 2) * TAPS_POOL)
                nc.vector.tensor_tensor(up[:, c % 3, TAPS - 1:UPW], bank[g % 2][:, 0:S], sg[:, c % 2, :],
                                        ALU.mult).then_inc(u_done, 1)

            gated(0)
            for c in range(KE + 1):
                if c < KE:
                    dve.wait_ge(u_done, j * KE + c + 1)
                    prev = [None, None]
                    for k in range(TAPS_DVE):
                        if k == 2 * TAPS_DVE // 3 and c + 1 < KE:
                            gated(c + 1)
                            dve_ahead(dve, n["vg"][c + 1][1])
                        a = k % 2
                        src = up[:, c % 3, k:k + S]
                        w = taps[:, j, k, c:c + 1]
                        if prev[a] is None:
                            ins = nc.vector.tensor_scalar(acca[:, a, :], src, w, None, ALU.mult)
                        else:
                            dve.wait_ge(step, prev[a])
                            ins = nc.vector.scalar_tensor_tensor(acca[:, a, :], src, w, acca[:, a, :], ALU.mult, ALU.add)
                        steps[0] += 1
                        ins.then_inc(step, 1)
                        prev[a] = steps[0]
                    dve.wait_ge(step, steps[0])
                    chain(dve, nc.vector.tensor_tensor(yb[:, c, :], acca[:, 0, :], acca[:, 1, :], ALU.add))
                if c >= 1:
                    dve.wait_ge(tap_done, (j * KE + c) * TAPS_POOL)
                    nc.vector.tensor_tensor(yb[:, c - 1, :], yb[:, c - 1, :], accp[:, (c - 1) % 2, :], ALU.add)\
                        .then_inc(conv_done, 1)
            dve.wait_ge(conv_done, j * KE + KE)
            dve_ahead(dve, n["z"][4][1])
            dve.wait_ge(mean_done, j + 1)
            for c in range(KE):
                nc.vector.scalar_tensor_tensor(yb[:, c, :], bank[7][:, 0:S], -1.0 / E, yb[:, c, :],
                                               ALU.mult, ALU.add).then_inc(dc_done, 1)
            dve.wait_ge(lstd_done, j + 1)
            chain(dve, nc.vector.reciprocal(rr[:, 0:S], std[:, 0:S]))
            for c in range(KE + 3):
                if c in Z_BESIDE:
                    dve_ahead(dve, n["z"][Z_BESIDE[c]][1])
                if c < KE:
                    nc.vector.tensor_tensor(yb[:, c, :], yb[:, c, :], rr[:, 0:S], ALU.mult).then_inc(dn_done, 1)
                if c >= 3:
                    y_low(dve, n["y0"] + c - 3, y_hi[:, c - 3, :], y_lo[:, c - 3, :])
            out_dve(dve, n)

        def conf_pe(pe, n):
            j = n["j"]
            rms_pe(pe, n["ph"])
            for c in range(KE + 3):
                if c < KE:
                    proj_T(pe, *n["vg"][c], c == 0, n["ph"])
                    if c % 4 == 3:
                        proj_T(pe, *n["z"][c // 4])
                if c == KE:
                    proj_T(pe, *n["z"][4])
                if c >= 3:
                    pe.wait_ge(conv_done, j * KE + c - 2)
                    mm = nc.tensor.matmul(bank[7][:, 0:S], ones, yb[:, c - 3, :], start=(c == 3), stop=(c == KE + 2))
            mm.then_inc(mean_done, 1)
            for c in range(KE):
                pe.wait_ge(sqd_done, j * KE + c + 1)
                nc.tensor.matmul(bank[6][:, 0:S], ones, sq4[:, c % 4, :], start=(c == 0),
                                 stop=(c == KE - 1)).then_inc(sqm_done, 1)
            for i in range(5, 8):
                proj_T(pe, *n["z"][i])
            out_pe(pe, n, y_hi, y_lo, KE, y_split, n["y0"])

        class Jobs:
            def __init__(self, name, jobs, o_done, o_base=0):
                self.jobs = jobs
                self.first = [sum(len(x["parts"]) for x in jobs[:i]) for i in range(len(jobs) + 1)]
                self.s_ready = sem(f"{name}_logits_ready")
                self.ttr_done = sem(f"{name}_bias_added")
                self.nm_done = sem(f"{name}_max_ready")
                self.exp_done = sem(f"{name}_exp_done")
                self.norm_done = sem(f"{name}_probs_ready")
                self.tr_done = sem(f"{name}_probs_transposed")
                self.pt_copied = sem(f"{name}_transposes_copied")
                self.pv_done = sem(f"{name}_values_summed")
                self.o_done, self.o_base = o_done, o_base

        BLOCKS = ((0, P), (P, 3 * P))

        def spans(part):
            return ((0, NCMP), (P, P + NCMP)) if part.get("cmp") else BLOCKS

        def qk_pe(pe, A, j, ready=None):
            job = A.jobs[j]
            for s, v in job.get("waits", []):
                pe.wait_ge(s, v)
            for i, part in enumerate(job["parts"]):
                p = A.first[j] + i
                wait(pe, A.ttr_done, 2 * (p - 1))
                b = bank[2 + p % 2]
                for tb, (c0, c1) in enumerate(spans(part)):
                    prods = [(part["q"][:, tb * P:(tb + 1) * P], part["k"][:, 0:c1 - c0])]
                    prods += [(l(tb), r(tb)) for l, r in part.get("more", [])]
                    for m, (l, r) in enumerate(prods):
                        mm = nc.tensor.matmul(b[:, c0:c1], l, r, start=(m == 0), stop=(m == len(prods) - 1))
                mm.then_inc(A.s_ready, 1)

        def scores_dve(dve, A, j):
            job = A.jobs[j]
            r = j % 3
            for i, part in enumerate(job["parts"]):
                p = A.first[j] + i
                dve.wait_ge(A.s_ready, p + 1)
                wait(dve, A.tr_done, p - 5)
                for tb, (c0, c1) in enumerate(spans(part)):
                    nc.vector.tensor_tensor_reduce(Lb[:, p % 6, c0:c1], bank[2 + p % 2][:, c0:c1], part["bias"](tb), 1.0,
                                                   -3.0e38, ALU.add, ALU.max, mstat[:, r, 3 * tb + i:3 * tb + i + 1])\
                        .then_inc(A.ttr_done, 1)
            dve.wait_ge(A.ttr_done, 2 * A.first[j + 1])
            n = len(job["parts"])
            m = mstat[:, r, :].rearrange("p (b i) -> p b i", b=2)[:, :, 0:n]
            d = nstat[:, r, :].rearrange("p (b i) -> p b i", b=2)[:, :, 0:n]
            if job.get("joint"):
                chain(dve, nc.vector.tensor_reduce(jstat[:, r, 0:2], m, AX, ALU.max))
                m, d = jstat[:, r, 0:2], nstat[:, r, 0:2]
            nc.vector.tensor_scalar(d, m, -1.0, 1e29, ALU.mult, ALU.min).then_inc(A.nm_done, 1)

        def exps_act(act, A, j):
            job = A.jobs[j]
            r = j % 3
            act.wait_ge(A.nm_done, j + 1)
            for i, part in enumerate(job["parts"]):
                p = A.first[j] + i
                for tb, (c0, c1) in enumerate(spans(part)):
                    nm = nstat[:, r, tb:tb + 1] if job.get("joint") else nstat[:, r, 3 * tb + i:3 * tb + i + 1]
                    nc.scalar.activation(Lb[:, p % 6, c0:c1], Lb[:, p % 6, c0:c1], ACT.Exp, bias=nm, scale=1.0,
                                         accum_out=sstat[:, r, 3 * tb + i:3 * tb + i + 1]).then_inc(A.exp_done, 1)

        def norm_dve(dve, A, j):
            job = A.jobs[j]
            r = j % 3
            n = len(job["parts"])
            dve.wait_ge(A.exp_done, 2 * A.first[j + 1])
            s = sstat[:, r, :].rearrange("p (b i) -> p b i", b=2)[:, :, 0:n]
            f = fstat[:, r, :].rearrange("p (b i) -> p b i", b=2)[:, :, 0:n]
            if job.get("joint"):
                chain(dve, nc.vector.tensor_reduce(jstat[:, r, 2:4], s, AX, ALU.add))
                s, f = jstat[:, r, 2:4], fstat[:, r, 0:2]
            chain(dve, nc.vector.tensor_scalar(s, s, 1e-30, None, ALU.max))
            chain(dve, nc.vector.reciprocal(f, s))
            if job.get("gate") is not None:
                chain(dve, nc.vector.tensor_tensor(f, f, job["gate"], ALU.mult))
            for i, part in enumerate(job["parts"]):
                p = A.first[j] + i
                for tb, (c0, c1) in enumerate(spans(part)):
                    fac = fstat[:, r, tb:tb + 1] if job.get("joint") else fstat[:, r, 3 * tb + i:3 * tb + i + 1]
                    nc.vector.tensor_scalar(Lb[:, p % 6, c0:c1], Lb[:, p % 6, c0:c1], fac, None, ALU.mult)\
                        .then_inc(A.norm_done, 1)

        def tr_pe(pe, A, j):
            for i, part in enumerate(A.jobs[j]["parts"]):
                p = A.first[j] + i
                pe.wait_ge(A.norm_done, 2 * p + 2)
                wait(pe, A.pt_copied, p - 1)
                b = bank[4 + p % 2]
                if part.get("cmp"):
                    for tb in range(TB):
                        mm = nc.tensor.transpose(b[0:NCMP, tb * P:(tb + 1) * P], Lb[:, p % 6, tb * P:tb * P + NCMP], ident)
                else:
                    for m in range(3):
                        mm = nc.tensor.transpose(b[:, m * P:(m + 1) * P], Lb[:, p % 6, m * P:(m + 1) * P], ident)
                mm.then_inc(A.tr_done, 1)

        def pt_act(act, A, j):
            for i, part in enumerate(A.jobs[j]["parts"]):
                p = A.first[j] + i
                act.wait_ge(A.tr_done, p + 1)
                wait(act, A.pv_done, p - 5)
                rows_, w = (NCMP, S) if part.get("cmp") else (P, 3 * P)
                nc.scalar.copy(PT[0:rows_, p % 6, 0:w], bank[4 + p % 2][0:rows_, 0:w]).then_inc(A.pt_copied, 1)

        def pv_pe(pe, A, j):
            job = A.jobs[j]
            tile, half, mw = job["tile"], job["half"], job["width"]
            for s, v in job.get("v_waits", []):
                pe.wait_ge(s, v)
            if half == 0:
                wait(pe, A.o_done, A.o_base + tile - 1 if tile >= 2 else 0)
            o = bank[6 + tile % 2][64 * half:64 * half + mw, :]
            n = len(job["parts"])
            for i, part in enumerate(job["parts"]):
                p = A.first[j] + i
                pe.wait_ge(A.pt_copied, p + 1)
                if part.get("cmp"):
                    mm = nc.tensor.matmul(o[:, 0:S], part["v"](0), PT[0:NCMP, p % 6, 0:S], start=(i == 0), stop=(i == n - 1))
                else:
                    nc.tensor.matmul(o[:, 0:S], part["v"](0), PT[:, p % 6, 0:S], start=(i == 0), stop=False)
                    mm = nc.tensor.matmul(o[:, P:S], part["v"](1), PT[:, p % 6, S:S + P], start=False, stop=(i == n - 1))
                mm.then_inc(A.pv_done, 1)

        fw = sg[0:FH, :, :]
        ssr = std[0:FH, :]
        rr_hi, rr_lo = (y_hi[0:FH, 2 * i:2 * i + 2, :].rearrange("p a t -> p (a t)") for i in range(2))
        id_r = y_hi[0:FH, 4, 0:FH]
        f_hi, f_lo = sem("f_hi"), sem("f_lo")

        cpos, cneg = zb[0:FH, KE, :], zb[0:FH, KE + 1, :]

        def sel_h(h, n):
            return ident[0:FH, h:h + 1].to_broadcast((FH, n))

        fox_jobs = []
        for h in range(FH):
            part = {"q": qk[:, h, 0, :], "k": qk[:, h, 1, :],
                    "more": [(lambda tb, h=h: sel_h(h, P), lambda tb: cneg[:, 0:(tb + 1) * P]),
                             (lambda tb: cpos[:, tb * P:(tb + 1) * P], lambda tb, h=h: sel_h(h, (tb + 1) * P))],
                    "bias": lambda tb: cst[:, C_MASK + P:C_MASK + S] if tb == 0 else cst[:, C_MASK:C_MASK + S],
                    "v": lambda sblk, h=h: vb[:, sblk, h * P:(h + 1) * P]}
            fox_jobs.append({"parts": [part], "tile": h, "half": 0, "width": P, "waits": [],
                             "v_waits": [(f_v, h // 2 + 1)]})
        fox_jobs[0]["waits"] = [(f_c, 4), (f_n, 2 * FH)]
        AF = Jobs("fox", fox_jobs, y_raw, fox["y0"])
        fsq = [scratch[:, 900 + 512 * i:900 + 512 * i + 512] for i in range(2)]

        def fox_act(act, n):
            act.wait_ge(skew_written, 64)
            rms_act(act, n["ph"])
            g, u = n["f"]
            act_ahead(act, u)
            group_done(act, u)
            nc.scalar.activation(fw[:, 0, :], bank[g % 2][0:FH, 0:S], ACT.Identity, bias=fb).then_inc(f_e, 1)
            act.wait_ge(f_e, 1)
            nc.scalar.activation(fw[:, 1, :], fw[:, 0, :], ACT.Abs).then_inc(f_e, 1)
            act.wait_ge(f_e, 2)
            nc.scalar.activation(fw[:, 1, :], fw[:, 1, :], ACT.Exp, scale=-1.0).then_inc(f_e, 1)
            act.wait_ge(f_e, 3)
            nc.scalar.activation(fw[:, 1, :], fw[:, 1, :], ACT.Ln, bias=1.0).then_inc(f_e, 1)
            for h, (g, u) in enumerate(n["qk"]):
                act_ahead(act, u)
                group_done(act, u)
                wait(act, f_ss, h - 1)
                nc.scalar.activation(fsq[h % 2], bank[g % 2][:, :], ACT.Square).then_inc(f_sq, 1)
                nc.scalar.copy(qk[:, h, :, :].rearrange("p a t -> p (a t)"), bank[g % 2][:, :]).then_inc(f_raw, 1)
            act.wait_ge(f_ss, FH)
            nc.scalar.activation(ssr, bank[7][0:FH, :], ACT.Sqrt, scale=1.0 / FD, bias=eps[0:FH, :]).then_inc(f_std, 1)
            nc.scalar.copy(id_r, ident[0:FH, 0:FH]).then_inc(f_hi, 1)
            act.wait_ge(f_rr, 1)
            nc.scalar.copy(rr_hi, rr[0:FH, :]).then_inc(f_hi, 1)
            for j in range(-3, FH + 1):
                if 0 <= j < FH:
                    exps_act(act, AF, j)
                if j in n["at"]:
                    kind, i = n["at"][j]
                    g, u = n[kind][i]
                    act_ahead(act, u)
                    group_done(act, u)
                    if kind == "z":
                        nc.scalar.activation(zb[:, 2 * i:2 * i + 2, :], bank[g % 2][:, :].rearrange("p (a t) -> p a t", t=S),
                                             ACT.Silu).then_inc(f_z, 1)
                    else:
                        nc.scalar.copy(vb[:, :, i * S:(i + 1) * S], bank[g % 2][:, :].rearrange("p (b n) -> p b n", b=TB))\
                            .then_inc(f_v, 1)
                if j >= 1:
                    pt_act(act, AF, j - 1)
                if j >= 3:
                    y_high(act, n["y0"] + j - 3, y_hi[:, j - 3, :])
            for h in (FH - 2, FH - 1):
                y_high(act, n["y0"] + h, y_hi[:, h, :])
            out_act(act, n)

        def fox_dve(dve, n):
            rms_dve(dve, n["ph"])
            dve_ahead(dve, n["f"][1])
            dve.wait_ge(f_e, 4)
            nc.vector.scalar_tensor_tensor(cpos, fw[:, 0, :], 0.0, fw[:, 1, :], ALU.min, ALU.subtract).then_inc(f_c, 1)
            dve.wait_ge(f_c, 1)
            nc.vector.tensor_tensor_scan(cneg, ones[0:FH, 0:1].to_broadcast((FH, S)), cpos, 0.0, ALU.mult, ALU.add).then_inc(f_c, 1)
            dve.wait_ge(f_c, 2)
            nc.vector.tensor_copy(cpos, cneg).then_inc(f_c, 1)
            dve.wait_ge(f_c, 3)
            nc.vector.tensor_scalar(cneg, cneg, -1.0, None, ALU.mult).then_inc(f_c, 1)
            for g, u in n["qk"]:
                dve_ahead(dve, u)
            dve.wait_ge(f_std, 1)
            nc.vector.reciprocal(rr[0:FH, :], ssr).then_inc(f_rr, 1)
            dve.wait_ge(f_hi, 2)
            nc.vector.tensor_tensor(rr_lo, rr[0:FH, :], rr_hi.bitcast(F32), ALU.subtract).then_inc(f_lo, 1)
            for h in range(FH):
                dve_ahead(dve, n["z"][1 + h // 8][1])
                dve.wait_ge(f_rb, h + 1)
                for a in range(2):
                    gain = gq[:, 0:1] if a == 0 else cols[:, FK:FK + 1]
                    nc.vector.scalar_tensor_tensor(qk[:, h, a, :], qk[:, h, a, :], gain, bank[2 + h % 2][:, a * S:(a + 1) * S],
                                                   ALU.mult, ALU.mult).then_inc(f_n, 1)
            for j in range(FH + 3):
                if j < FH:
                    if j in n["at"]:
                        kind, i = n["at"][j]
                        lo_dve_to(dve, last(n[kind][i][1]))
                    scores_dve(dve, AF, j)
                if 1 <= j <= FH:
                    norm_dve(dve, AF, j - 1)
                if j >= 3:
                    y_low(dve, n["y0"] + j - 3, y_hi[:, j - 3, :], y_lo[:, j - 3, :])
                if 2 <= j < FH + 2:
                    h = j - 2
                    dve.wait_ge(AF.pv_done, h + 1)
                    nc.vector.tensor_tensor(y_slot(dve, n["y0"] + h), bank[6 + h % 2][:, 0:S], zb[:, h, :], ALU.mult).then_inc(y_raw, 1)
            out_dve(dve, n)

        def fox_pe(pe, n):
            rms_pe(pe, n["ph"])
            g, u = n["f"]
            proj_T(pe, g, u, True, n["ph"])

            def sums(h):
                pe.wait_ge(f_sq, h + 1)
                nc.tensor.matmul(bank[7][0:FH, :], cst[:, C_E1 + 15 - h:C_E1 + 15 - h + FH], fsq[h % 2],
                                 start=(h == 0), stop=(h == FH - 1)).then_inc(f_ss, 1)

            for h, (g, u) in enumerate(n["qk"]):
                proj_T(pe, g, u)
                if h >= 1:
                    sums(h - 1)
            proj_T(pe, *n["z"][0])
            sums(FH - 1)
            proj_T(pe, *n["z"][1])
            for h in range(FH):
                if h == 8:
                    proj_T(pe, *n["z"][2])
                fox_rb(pe, h)
            for j in range(FH + 2):
                if j < FH:
                    qk_pe(pe, AF, j)
                    if j in n["at"]:
                        kind, i = n["at"][j]
                        (proj_N if kind == "v" else proj_T)(pe, *n[kind][i])
                if 1 <= j <= FH:
                    tr_pe(pe, AF, j - 1)
                if j >= 2:
                    pv_pe(pe, AF, j - 2)
            out_pe(pe, n, y_hi, y_lo, KE, y_split, n["y0"])

        def fox_rb(pe, h):
            if h == 0:
                pe.wait_ge(f_lo, 1)
            wait(pe, f_n, 2 * (h - 1))
            row = id_r[:, h:h + 1].to_broadcast((FH, P))
            nc.tensor.matmul(bank[2 + h % 2][:, :], row, rr_hi, start=True, stop=False)
            nc.tensor.matmul(bank[2 + h % 2][:, :], row, rr_lo, start=False, stop=True).then_inc(f_rb, 1)

        cup = scratch[:, 0:2 * (S + 2)].rearrange("p (r w) -> p r w", w=S + 2)
        ccg = scratch[:, 600:600 + 2 * S].rearrange("p (r w) -> p r w", w=S)
        csz = scratch[:, 1200:1200 + 2 * S].rearrange("p (r w) -> p r w", w=S)
        cac = scratch[:, 1800:1800 + 2 * S].rearrange("p (r w) -> p r w", w=S)

        def short_act(act, n):
            rms_act(act, n["ph"])
            for c in range(KE):
                g, u = n["uc"][c]
                act_ahead(act, u)
                group_done(act, u)
                wait(act, c_cu, c - 1)
                nc.scalar.copy(ccg[:, c % 2, :], bank[g % 2][:, S:2 * S]).then_inc(c_cg, 1)
                g, u = n["bz"][c]
                act_ahead(act, u)
                group_done(act, u)
                wait(act, y_raw, n["y0"] + c - 1 if c >= 2 else 0)
                nc.scalar.activation(csz[:, c % 2, :], bank[g % 2][:, S:2 * S], ACT.Silu).then_inc(c_sz, 1)
                if c >= 1:
                    y_high(act, n["y0"] + c - 1, y_hi[:, c - 1, :])
            y_high(act, n["y0"] + KE - 1, y_hi[:, KE - 1, :])
            out_act(act, n)

        def short_dve(dve, n):
            for r in range(2):
                chain(dve, nc.vector.memset(cup[:, r, 0:2], 0.0))
            rms_dve(dve, n["ph"])
            for c in range(KE):
                g, u = n["uc"][c]
                dve_ahead(dve, u)
                dve.wait_ge(c_cg, c + 1)
                nc.vector.tensor_tensor(cup[:, c % 2, 2:S + 2], bank[g % 2][:, 0:S], ccg[:, c % 2, :], ALU.mult).then_inc(c_cu, 1)
                dve.wait_ge(c_cu, c + 1)
                chain(dve, nc.vector.tensor_scalar(cac[:, c % 2, :], cup[:, c % 2, 0:S], short_w(0, c), None, ALU.mult))
                for k in range(1, SHORT):
                    chain(dve, nc.vector.scalar_tensor_tensor(cac[:, c % 2, :], cup[:, c % 2, k:k + S], short_w(k, c),
                                                              cac[:, c % 2, :], ALU.mult, ALU.add))
                g, u = n["bz"][c]
                dve_ahead(dve, u)
                dve.wait_ge(c_sz, c + 1)
                chain(dve, nc.vector.tensor_tensor(cac[:, c % 2, :], cac[:, c % 2, :], csz[:, c % 2, :], ALU.mult))
                nc.vector.tensor_tensor(y_slot(dve, n["y0"] + c), bank[g % 2][:, 0:S], cac[:, c % 2, :], ALU.mult).then_inc(y_raw, 1)
                if c >= 1:
                    y_low(dve, n["y0"] + c - 1, y_hi[:, c - 1, :], y_lo[:, c - 1, :])
            y_low(dve, n["y0"] + KE - 1, y_hi[:, KE - 1, :], y_lo[:, KE - 1, :])
            out_dve(dve, n)

        def short_pe(pe, n):
            rms_pe(pe, n["ph"])
            for c in range(KE):
                proj_T(pe, *n["uc"][c], c == 0, n["ph"])
                proj_T(pe, *n["bz"][c])
            out_pe(pe, n, y_hi, y_lo, KE, y_split, n["y0"])

        msq = [scratch[:, 2304 + 512 * i:2304 + 512 * i + 512] for i in range(2)]
        RAW_OF = {}
        for i, (kind, g, u) in enumerate(mixers["in"]):
            if kind == "raw":
                RAW_OF[i] = len(RAW_OF)
        normed = [i for i in RAW_OF if i != 1]
        IK, IQ = qk[:, 0, 1, :], qk[:, 1, :, :]
        AQ, BQ, KS, KW, CQ, CK = 2, 4, 6, 7, 8, 11
        V_A, V_S, V_IW, V_BG, V_W, V_C = 0, HD, HD + P, HD + P + IDX_H, 220, 348
        NAT_AT = {2: 0, 17: V_W, 18: V_C, 19: V_C + S, 20: V_C + 2 * S}
        vflat = vb_flat[:, 0:TB * 1116].rearrange("p (b n) -> p b n", b=TB)
        rest = vb_flat[:, TB * 1116:TB * E]
        cmp_in = rest[:, 0:2 * S].rearrange("p (g t) -> p g t", g=B_G)
        cblk = [rest[:, 512 + 480 * i:512 + 480 * (i + 1)].rearrange("p (l g n) -> p l g n", l=LC, g=B_G) for i in range(2)]
        kcT = rest[:, 1472:1502]
        vcT = rest[:, 1502:1532]
        vcN = rest[0:NCMP, 1532:1532 + 2 * HD].rearrange("p (g e) -> p g e", g=B_G)
        kraw, ksq = rest[:, 1660:1690], rest[:, 1690:1720]
        kstd = rest[:, 1720:1750]
        cw = wide[:, 0:12 * S]
        cwk = cw[:, 0:LC * P].rearrange("p (l e) -> p l e", l=LC)
        cwv = cw[:, LC * P:LC * P + LC * HD].rearrange("p (l e) -> p l e", l=LC)
        keep = wide[:, 28 * S:32 * S]
        selr = scratch[0:32, 0:NORMED * P]
        isc = keep[:, 0:384]
        rel4 = keep[:, 384:384 + 512].rearrange("p (r w) -> p r w", w=256)
        amask = convw[:, 0:384]
        i_s, i_r, i_a, i_top, i_m = sem("i_s"), sem("i_r"), sem("i_a"), sem("i_top"), sem("i_m")
        k_in, k_blk, k_mm, k_c, k_v = sem("k_in"), sem("k_blk"), sem("k_mm"), sem("k_c"), sem("k_v")
        k_fin = sem("k_fin")
        g_s = sem("g_s")

        def q_of(s0, h):
            half = h % 2
            return qk[64 * half:64 * half + 64, s0 + h // 4, (h // 2) % 2, :]

        def half_of(ap3, h):
            return ap3[64 * (h % 2):64 * (h % 2) + 64]

        def bias_of(h):
            return lambda tb: T[:, h, P:S] if tb == 0 else T[:, h, :]

        jobs = []
        for hh in range(C_SLOTS):
            parts = []
            for gi in range(3):
                h = gi * C_SLOTS + hh
                parts.append({"q": q_of(CQ, h), "k": q_of(CK, h), "bias": bias_of(A_H + B_H + h),
                              "v": lambda sblk, h=h: vflat[:, sblk, V_C + h * HD:V_C + (h + 1) * HD]})
            jobs.append({"parts": parts, "joint": True, "tile": hh // 2, "half": hh % 2, "width": HD})
        for h in range(B_H):
            g = h // (B_H // B_G)
            parts = [{"cmp": True, "q": q_of(BQ, h), "k": half_of(kcT, h)[:, g * NCMP:(g + 1) * NCMP],
                      "bias": lambda tb: cst[:, C_CMP + tb * NCMP:C_CMP + (tb + 1) * NCMP],
                      "v": lambda sblk, g=g: vcN[:, g, :]},
                     {"q": q_of(BQ, h), "k": half_of(qk[:, KS, g, :], h), "bias": bias_of(A_H + h),
                      "v": lambda sblk, g=g: vflat[:, sblk, V_S + g * HD:V_S + (g + 1) * HD]},
                     {"q": q_of(BQ, h), "k": half_of(qk[:, KW, g, :], h), "bias": bias_of(A_H + h),
                      "v": lambda sblk, g=g: vflat[:, sblk, V_W + g * HD:V_W + (g + 1) * HD]}]
            jobs.append({"parts": parts, "gate": gate_s[:, :, 3 * h:3 * h + 3], "tile": 2 + h // 2, "half": h % 2, "width": HD})
        for h in range(A_H):
            part = {"q": q_of(AQ, h), "k": half_of(qk[:, 0, 0, :], h), "bias": bias_of(h),
                    "more": [(lambda tb: ident, lambda tb: amask[:, 0:P] if tb == 0 else amask[:, P:3 * P])],
                    "v": lambda sblk: vflat[:, sblk, V_A:V_A + HD]}
            jobs.append({"parts": [part], "tile": 6 + h // 2, "half": h % 2, "width": HD})
        NJ = len(jobs)
        jobs[0]["waits"] = [(m_n, NORMED), (T_loaded, 16)]
        jobs[C_SLOTS]["waits"] = [(k_fin, 1)]
        jobs[C_SLOTS]["v_waits"] = [(k_v, 3)]
        jobs[C_SLOTS + B_H]["waits"] = [(i_m, 2)]
        AM = Jobs("m", jobs, sem("m_output_used"))

        def filler_at(j):
            def before(j):
                return max(0, (j - C_SLOTS) * 12 // (NJ - C_SLOTS))

            return range(before(j), before(j + 1))

        def mixers_act(act, n):
            rms_act(act, n["ph"])
            act.dma_start(selr, t["sel"]).then_inc(sel_loaded, 16)
            w0 = t["nsa_cmp_w_2"][0]
            for i in range(2):
                act.dma_start(cwk[:, :, i * HD:(i + 1) * HD], w0[0].rearrange("(l q) d e -> (q d) l e", q=2)).then_inc(cmpw_loaded, 16)
            act.dma_start(cwv, w0[1].rearrange("(l q) d e -> (q d) l e", q=2)).then_inc(cmpw_loaded, 16)
            count = {"sq": 0, "cmp": 0}
            for i, (kind, g, u) in enumerate(n["in"]):
                b = bank[g % 2]
                act_ahead(act, u)
                group_done(act, u)
                if kind == "raw":
                    if i in normed:
                        q = count["sq"]
                        wait(act, m_ss, q - 1)
                        nc.scalar.activation(msq[q % 2], b[:, :], ACT.Square).then_inc(m_sq, 1)
                        count["sq"] += 1
                    nc.scalar.copy(qk[:, RAW_OF[i], :, :].rearrange("p a t -> p (a t)"), b[:, :]).then_inc(m_raw, 1)
                elif kind == "nat":
                    wn = units[u][0]
                    src = b[:, :].rearrange("p (b n) -> p b n", b=TB)[:, :, 0:wn]
                    nc.scalar.copy(vflat[:, :, NAT_AT[i]:NAT_AT[i] + wn], src).then_inc(m_raw, 1)
                else:
                    q = count["cmp"]
                    wait(act, k_blk, q)
                    bb = b[:, :].rearrange("p (g t) -> p g t", g=B_G)
                    nc.scalar.copy(cmp_in[0:64, :, :], bb[0:64, :, :]).then_inc(k_in, 1)
                    nc.scalar.copy(cmp_in[64:P, :, 0:S - 1], bb[64:P, :, 1:S]).then_inc(m_raw, 1)
                    count["cmp"] += 1
                if i == 2:
                    act.wait_ge(m_raw, 3)
                    nc.scalar.activation(gate_s, vflat[:, :, V_BG:V_BG + 24], ACT.Sigmoid).then_inc(g_s, 1)
                if 5 <= i < 9:
                    for m in range(2 * (i - 5), 2 * (i - 4)):
                        act.wait_ge(i_s, m + 1)
                        wait(act, i_a, m - 1)
                        w = P * (m // 4 + 1)
                        nc.scalar.activation(rel4[:, m % 2, 0:w], bank[2 + m % 2][:, 0:w], ACT.Relu).then_inc(i_r, 1)
                if i == 9:
                    act.wait_ge(k_mm, 1)
                    nc.scalar.copy(kraw, bank[4][:, 0:30]).then_inc(k_c, 1)
                    nc.scalar.activation(ksq, bank[4][:, 0:30], ACT.Square).then_inc(k_c, 1)
                    act.wait_ge(k_mm, 2)
                    nc.scalar.copy(vcT[0:64, :], bank[5][0:64, 0:30]).then_inc(k_v, 1)
                if i == 16:
                    act.wait_ge(i_m, 2)
                    act.dma_start(T[:, :, :], bass.AP(tensor=skew.tensor, offset=skew.offset + P - 1,
                                                      ap=[[TABLE - 1, P], [P * TABLE, HEADS2], [1, S]])).then_inc(T_loaded, 16)
                if i == 11:
                    for g2 in range(2):
                        act.wait_ge(k_mm, 5)
                        nc.scalar.copy(vcN[:, g2, :], bank[5][0:NCMP, 64 + 64 * g2:128 + 64 * g2]).then_inc(k_v, 1)
            act.wait_ge(m_ss, NORMED)
            nc.scalar.activation(std[0:32, :], bank[7][0:32, :], ACT.Sqrt, scale=1.0 / HD, bias=eps[0:32, :]).then_inc(m_std, 1)
            nc.scalar.activation(kstd, bank[4][:, 64:94], ACT.Sqrt, scale=1.0 / HD, bias=eps).then_inc(m_std, 1)
            for j in range(NJ + 1):
                if j < NJ:
                    exps_act(act, AM, j)
                    for f in filler_at(j):
                        g, u = n["mix"][f]
                        act_ahead(act, u)
                        group_done(act, u)
                        nc.scalar.copy(mixt(2 * f), bank[g % 2][:, :].rearrange("p (a t) -> p a t", t=S)).then_inc(m_mix, 1)
                if j >= 1:
                    pt_act(act, AM, j - 1)
            act_ahead(act, n["mix"][-1][1])
            for i in (6, 8, 2, 4, 0):
                act.wait_ge(AM.o_done, 10)
                nc.scalar.copy(y_hi[:, i:i + 2, :], oT[:, i:i + 2, :]).then_inc(oh_done, 1)
            act.wait_ge(m_mix, 12)
            for d in range(0, KD, 2):
                for i in range(3):
                    nc.scalar.activation(mixt(8 * i + d), mixt(8 * i + d), ACT.Sigmoid).then_inc(mix_s, 1)
            for d2, br in enumerate(n["br"]):
                for g, us in br:
                    act_ahead(act, us[-1])
                if d2 >= 1:
                    mix_high(act, d2 - 1)
            mix_high(act, 3)
            out_act(act, n)

        def mix_high(act, d2):
            act.wait_ge(mixed, 2 * d2 + 2)
            nc.scalar.copy(m_hl[:, 2 * d2:2 * d2 + 2, :], mixt(2 * d2)).then_inc(mh_done, 1)

        def mix_low(dve, d2):
            dve.wait_ge(mh_done, d2 + 1)
            nc.vector.tensor_tensor(m_hl[:, KD + 2 * d2:KD + 2 * d2 + 2, :], mixt(2 * d2),
                                    m_hl[:, 2 * d2:2 * d2 + 2, :].bitcast(F32), ALU.subtract).then_inc(ml_done, 2)

        def mixers_dve(dve, n):
            rms_dve(dve, n["ph"])
            for q in range(2):
                dve.wait_ge(m_raw, 4 + q)
                src = bass_view(cmp_in)
                pos = cols[:, POS + LC * q:POS + LC * (q + 1)]
                for g in range(B_G):
                    i = nc.vector.tensor_tensor(cblk[q][:, :, g, :].rearrange("p l n -> p n l"), src[g],
                                                pos.unsqueeze(1).to_broadcast((P, NCMP, LC)), ALU.add)
                    if g == 0:
                        chain(dve, i)
                    else:
                        i.then_inc(k_blk, 1)
            for m in range(8):
                tb, h = divmod(m, IDX_H)
                w = P * (tb + 1)
                at = isc[:, 0:P] if tb == 0 else isc[:, P:3 * P]
                dve.wait_ge(i_r, m + 1)
                if h:
                    dve.wait_ge(i_a, m)
                if h == 0:
                    nc.vector.tensor_scalar(at, rel4[:, m % 2, 0:w], vflat[:, tb, V_IW:V_IW + 1], None, ALU.mult).then_inc(i_a, 1)
                else:
                    nc.vector.scalar_tensor_tensor(at, rel4[:, m % 2, 0:w], vflat[:, tb, V_IW + h:V_IW + h + 1], at,
                                                   ALU.mult, ALU.add).then_inc(i_a, 1)
            dve.wait_ge(i_a, 8)
            for tb in range(TB):
                at = isc[:, 0:P] if tb == 0 else isc[:, P:3 * P]
                mk = cst[:, C_MASK + P:C_MASK + S] if tb == 0 else cst[:, C_MASK:C_MASK + S]
                nc.vector.tensor_tensor(at, at, mk, ALU.add).then_inc(i_a, 1)
            dve.wait_ge(i_a, 10)
            done = [0, 0]
            cnt = 0
            for r in range(TOPK // 8):
                for tb in range(TB):
                    at = isc[:, 0:P] if tb == 0 else isc[:, P:3 * P]
                    wait(dve, i_top, done[tb])
                    nc.vector.max(best[:, tb, :], at).then_inc(i_top, 1)
                    cnt += 1
                    done[tb] = cnt
                for tb in range(TB):
                    at = isc[:, 0:P] if tb == 0 else isc[:, P:3 * P]
                    wait(dve, i_top, done[tb])
                    nc.vector.match_replace(at, best[:, tb, :], at, -3.0e38).then_inc(i_top, 1)
                    cnt += 1
                    done[tb] = cnt
            dve.wait_ge(i_top, cnt)
            for tb in range(TB):
                at = slice(0, P) if tb == 0 else slice(P, 3 * P)
                nc.vector.tensor_scalar(amask[:, at], isc[:, at], -2.0e38, NEG, ALU.is_gt, ALU.mult).then_inc(i_m, 1)
            dve.wait_ge(m_std, 1)
            nc.vector.reciprocal(rr[0:32, :], std[0:32, :]).then_inc(m_rr, 1)
            dve.wait_ge(m_std, 2)
            chain(dve, nc.vector.reciprocal(kstd, kstd))
            dve.wait_ge(k_c, 2)
            nc.vector.scalar_tensor_tensor(kcT, kraw, cols[:, QK2 + 3:QK2 + 4], kstd, ALU.mult, ALU.mult).then_inc(k_fin, 1)
            for q, i in enumerate(normed):
                dve.wait_ge(m_rb, q + 1)
                s0 = RAW_OF[i]
                gain = {0: cols[:, QK2 + 1:QK2 + 2], AQ: gq[:, 1:2], BQ: gq[:, 2:3], KS: cols[:, QK2 + 3:QK2 + 4],
                        CQ: gq[:, 3:4], CK: cols[:, QK2 + 5:QK2 + 6]}
                gcol = gain[0 if s0 == 0 else AQ if s0 < BQ else BQ if s0 < KS else KS if s0 < CQ else CQ if s0 < CK else CK]
                wd = S if s0 == 0 else 2 * S
                flat = qk[:, s0, :, :].rearrange("p a t -> p (a t)")[:, 0:wd]
                nc.vector.scalar_tensor_tensor(flat, flat, gcol, bank[2 + q % 2][:, 0:wd], ALU.mult, ALU.mult).then_inc(m_n, 1)
            dve.wait_ge(g_s, 1)
            for j in range(NJ + 2):
                if j < NJ:
                    for f in filler_at(j):
                        lo_dve_to(dve, last(n["mix"][f][1]) + 1)
                    scores_dve(dve, AM, j)
                if 1 <= j <= NJ:
                    norm_dve(dve, AM, j - 1)
                if j >= 2 and jobs[j - 2]["half"] == 1:
                    tile = jobs[j - 2]["tile"]
                    dve.wait_ge(AM.pv_done, AM.first[j - 1])
                    nc.vector.tensor_copy(oT[:, tile, :], bank[6 + tile % 2][:, 0:S]).then_inc(AM.o_done, 1)
            lo_dve_to(dve, last(n["br"][0][0][1][0]) + 1)
            for i, t0 in enumerate((6, 8, 2, 4, 0)):
                dve.wait_ge(oh_done, i + 1)
                nc.vector.tensor_tensor(h_lo[:, t0:t0 + 2, :], oT[:, t0:t0 + 2, :], y_hi[:, t0:t0 + 2, :].bitcast(F32),
                                        ALU.subtract).then_inc(ol_done, 1)
            for d2, br in enumerate(n["br"]):
                d = 2 * d2
                for i, (g, us) in enumerate(br):
                    dve_ahead(dve, us[-1])
                    group_done(dve, us[-1])
                    dve.wait_ge(mix_s, 3 * d2 + i + 1)
                    gt = mixt(8 * i + d)
                    nc.vector.tensor_tensor(gt, gt, bank[g % 2][:, :].rearrange("p (a t) -> p a t", t=S), ALU.mult).then_inc(br_used, 1)
                dve.wait_ge(br_used, 3 * d2 + 3)
                g0, g1, g2 = (mixt(8 * i + d) for i in range(3))
                chain(dve, nc.vector.tensor_tensor(g0, g0, g1, ALU.add))
                nc.vector.tensor_tensor(g0, g0, g2, ALU.add).then_inc(mixed, 2)
                if d2 >= 1:
                    mix_low(dve, d2 - 1)
            mix_low(dve, 3)
            out_dve(dve, n)

        def bass_view(ap):
            got = []
            for g in range(B_G):
                a = ap[:, g, 0:S]
                got.append(bass.AP(tensor=a.tensor, offset=a.offset, ap=[list(a.ap[0]), [16, NCMP], [2, LC]]))
            return got

        def mixers_pe(pe, n):
            rms_pe(pe, n["ph"])

            def sums(q):
                pe.wait_ge(m_sq, q + 1)
                nc.tensor.matmul(bank[7][0:32, :], cst[:, C_E2 + 30 - 2 * q:C_E2 + 62 - 2 * q], msq[q % 2],
                                 start=(q == 0), stop=(q == NORMED - 1)).then_inc(m_ss, 1)

            pend = []
            q = 0
            for i, (kind, g, u) in enumerate(n["in"]):
                if kind == "nat":
                    proj_N(pe, g, u)
                else:
                    proj_T(pe, g, u, i == 0, n["ph"])
                while pend:
                    sums(pend.pop())
                if i in normed:
                    pend.append(q)
                    q += 1
                if 4 <= i < 8:
                    if i == 4:
                        pe.wait_ge(m_raw, 2)
                    for m in range(2 * (i - 4), 2 * (i - 3)):
                        tb, h = divmod(m, IDX_H)
                        wait(pe, i_r, m - 1)
                        half = h % 2
                        mm = nc.tensor.matmul(bank[2 + m % 2][:, 0:P * (tb + 1)], IQ[64 * half:64 * half + 64, h // 2, tb * P:(tb + 1) * P],
                                              IK[64 * half:64 * half + 64, 0:P * (tb + 1)], start=True, stop=True)
                        mm.then_inc(i_s, 1)
                if i == 8:
                    pe.wait_ge(cmpw_loaded, 48)
                    pe.wait_ge(k_blk, 2)
                    for l in range(LC):
                        mm = nc.tensor.matmul(bank[4][:, 0:30], cwk[:, l, :], cblk[0][:, l, :, :].rearrange("p g n -> p (g n)"),
                                              start=(l == 0), stop=(l == LC - 1))
                    mm.then_inc(k_mm, 1)
                    for l in range(LC):
                        mm = nc.tensor.matmul(bank[5][0:64, 0:30], cwv[:, l, :], cblk[1][:, l, :, :].rearrange("p g n -> p (g n)"),
                                              start=(l == 0), stop=(l == LC - 1))
                    mm.then_inc(k_mm, 1)
                if i == 10:
                    pe.wait_ge(k_c, 2)
                    nc.tensor.matmul(bank[4][:, 64:94], blk64, ksq, start=True, stop=True).then_inc(k_mm, 1)
                    pe.wait_ge(k_v, 1)
                    for g2 in range(B_G):
                        nc.tensor.transpose(bank[5][0:NCMP, 64 + 64 * g2:128 + 64 * g2], vcT[0:64, g2 * NCMP:(g2 + 1) * NCMP],
                                            ident[0:64, 0:64]).then_inc(k_mm, 1)
            while pend:
                sums(pend.pop())
            for q in range(NORMED):
                if q == 0:
                    pe.wait_ge(m_rr, 1)
                    pe.wait_ge(sel_loaded, 16)
                wait(pe, m_n, q - 1)
                nc.tensor.matmul(bank[2 + q % 2][:, :], selr[:, q * P:(q + 1) * P], rr[0:32, :],
                                 start=True, stop=True).then_inc(m_rb, 1)
            for j in range(NJ + 2):
                if j < NJ:
                    qk_pe(pe, AM, j)
                    for f in filler_at(j):
                        proj_T(pe, *n["mix"][f])
                if 1 <= j <= NJ:
                    tr_pe(pe, AM, j - 1)
                if j >= 2:
                    pv_pe(pe, AM, j - 2)
            first = (6, 2, 0)
            ready = (2, 4, 5)
            for d2, br in enumerate(n["br"]):
                for i, (g, us) in enumerate(br):
                    b = take_bank(pe, g)
                    pe.wait_ge(ol_done, ready[i])
                    for a, u in enumerate(us):
                        h = last(u)
                        split_ready(pe, h)
                        wh, wl = piece(whi, h), piece(wlo, h)
                        mm = products(b[:, a * S:(a + 1) * S],
                                      [((wh[:, k, :], wl[:, k, :]), (y_hi[:, first[i] + k, :], h_lo[:, first[i] + k, :]))
                                       for k in range((4, 4, 2)[i])])
                        mm.then_inc(half_done, 1)
            out_pe(pe, n, m_hl, m_hl[:, KD:2 * KD, :], KD, ml_done)

        def ffn_act(act, n):
            rms_act(act, n["ph"])
            for i, (g, u) in enumerate(n["gu"]):
                act_ahead(act, u)
                group_done(act, u)
                wait(act, y_raw, n["y0"] + i - 1 if i >= 2 else 0)
                nc.scalar.activation(sg[:, i % 2, :], bank[g % 2][:, 0:S], ACT.Silu).then_inc(h_silu, 1)
                if i >= 1:
                    y_high(act, n["y0"] + i - 1, y_lo[:, i - 1, :])
            y_high(act, n["y0"] + KF - 1, y_lo[:, KF - 1, :])
            out_act(act, n)

        def ffn_dve(dve, n):
            rms_dve(dve, n["ph"])
            for i, (g, u) in enumerate(n["gu"]):
                dve_ahead(dve, u)
                dve.wait_ge(h_silu, i + 1)
                nc.vector.tensor_tensor(y_slot(dve, n["y0"] + i), bank[g % 2][:, S:2 * S], sg[:, i % 2, :], ALU.mult).then_inc(y_raw, 1)
                if i >= 1:
                    y_low(dve, n["y0"] + i - 1, y_lo[:, i - 1, :], h_lo[:, i - 1, :])
            y_low(dve, n["y0"] + KF - 1, y_lo[:, KF - 1, :], h_lo[:, KF - 1, :])
            out_dve(dve, n)

        def ffn_pe(pe, n):
            rms_pe(pe, n["ph"])
            for i, (g, u) in enumerate(n["gu"]):
                proj_T(pe, g, u, i == 0, n["ph"])
            out_pe(pe, n, y_lo, h_lo, KF, y_split, n["y0"])

        row_src = [("a_norm", 0, 0, 16), ("b_norm", 0, 16, 8), ("c_norm", 0, 24, 8), ("norm1_g_2", 0, 32, 8), ("norm2_g_2", 0, 40, 8)]

        SETUP_LOADS = 27
        block = ctx.enter_context(nc.Block())

        @block.sync
        def _(sp):
            n = [0]

            def load(dst, src):
                sp.dma_start(dst, src).then_inc(setup_loaded, 16)
                n[0] += 1

            load(xnat, t["x"][0].rearrange("(b p) d -> p b d", p=P))
            load(cst[:, :], t["cst"])
            for name, r, r0, nr in row_src:
                load(rows[r0:r0 + nr, r, :], t[name].rearrange("a (k p) -> (a k) p", p=P))
            load(rows[48:49, 0, :], t["b_q_norm"])
            load(rows[49:50, 0, :], t["b_k_norm"])
            for i in range(2):
                load(rows[50:56, 0, i * HD:(i + 1) * HD], t["qk_norm_g_2"][0])
            load(rows[56:88, 0, :], t["nsa_cmp_pos_2"][0].rearrange("w (l q) d -> (w l) (q d)", q=2))
            for i, name in enumerate(("a_conv_b", "a_ln_g", "a_ln_b")):
                load(rows[32 * i:32 * i + 32, 1, :], t[name].rearrange("a (k p) -> (a k) p", p=P))
            load(rows[0:48, 2, :], t["c_conv_w"][0].rearrange("a (k p) -> (a k) p", p=P))
            flat = t["a_conv_w"].rearrange("j a (k p) -> (j a k) p", p=P)
            for i in range(8):
                load(rows[0:124, 3 + i, :], flat[124 * i:124 * i + 124, :])
            load(hot, t["hot"])
            load(small[0:32, 224:224 + HEADS2], t["rel_bias_2"])
            load(fb, t["b_f_bias"].rearrange("a h -> h a"))
            assert n[0] == SETUP_LOADS
            for u, (_, parts) in enumerate(units):
                if u >= RING:
                    h = last(u - RING)
                    if is_split(h):
                        sp.wait_ge(hi_done, n_hi[h])
                        wait(sp, lo_dve, n_dve(h))
                        wait(sp, lo_pool, n_hi[h] - n_dve(h))
                    else:
                        sp.wait_ge(half_done, h + 1)
                for nk, at, width, src in parts:
                    sp.dma_start(raw(u, nk)[:, :, at:at + width], src).then_inc(unit_loaded[u % RING], 16)

        @block.gpsimd
        def _(pool):
            nc.gpsimd.memset(eps, EPS).then_inc(set_pool, 1)
            pool.wait_ge(set_pool, 1)
            nc.gpsimd.memset(small[32:33, 224:224 + HEADS2], 1.0).then_inc(set_pool, 1)
            conf_pool(pool, conf0)
            lo_pool_to(pool, last(short["out"][-1][1][-1]))
            conf_pool(pool, conf1)
            lo_pool_to(pool, len(halves) - 1)

        ROWS_OF = [88, 96, 48] + [124] * 8

        @block.tensor
        def _(pe):
            pe.wait_ge(setup_loaded, 16 * SETUP_LOADS)
            pe.wait_ge(set_pool, 2)
            for i in range(4):
                for a in range(2):
                    for tb in range(TB):
                        k = 2 * i + a
                        mm = nc.tensor.transpose(bank[i][:, a * S + tb * P:a * S + (tb + 1) * P], xnat[:, tb, k * P:(k + 1) * P], ident)
                mm.then_inc(set_done, 1)
            for i in range(11):
                if i >= 4:
                    pe.wait_ge(set_used, i - 3)
                nr = ROWS_OF[i]
                nc.tensor.transpose(bank[4 + i % 4][:, 0:nr], rows[0:nr, i, :], ident[0:nr, 0:nr]).then_inc(set_done, 1)
            for v, (h0, nh) in enumerate(((0, 16), (16, 4), (20, 4), (24, 4))):
                if v == 0:
                    pe.wait_ge(x_done, 4)
                nc.tensor.matmul(bank[v][0:nh, 0:TABLE], small[0:33, 224 + h0:224 + h0 + nh], hot[:, v * TABLE:(v + 1) * TABLE],
                                 start=True, stop=True).then_inc(tab_done, 1)
            pe.wait_ge(set_dve, 5)
            pe.wait_ge(tab_copied, 4)
            conf_pe(pe, conf0)
            fox_pe(pe, fox)
            short_pe(pe, short)
            conf_pe(pe, conf1)
            mixers_pe(pe, mixers)
            ffn_pe(pe, ffn)
            for i in range(4):
                pe.wait_ge(x_done, 4 * NPH + i + 1)
                for a in range(2):
                    for tb in range(TB):
                        k = 2 * i + a
                        mm = nc.tensor.transpose(bank[2 + i][:, a * S + tb * P:a * S + (tb + 1) * P], xT[:, k, tb * P:(tb + 1) * P], ident)
                mm.then_inc(set_done, 1)

        @block.vector
        def _(dve):
            for i in range(4):
                dve.wait_ge(set_done, i + 1)
                nc.vector.tensor_copy(xT[:, 2 * i:2 * i + 2, :], bank[i][:, :].rearrange("p (a t) -> p a t", t=S)).then_inc(x_done, 1)
            for i in range(11):
                dve.wait_ge(set_done, 5 + i)
                nr = ROWS_OF[i]
                if i < 3:
                    dst = cols[:, (0, 88, 184)[i]:(0, 88, 184)[i] + nr]
                else:
                    dst = convw[:, 124 * (i - 3):124 * (i - 2)]
                nc.vector.tensor_copy(dst, bank[4 + i % 4][:, 0:nr]).then_inc(set_used, 1)
            dve.wait_ge(set_used, 11)
            for i, (src, scale) in enumerate(((FQ, FD ** -0.5), (QK2, HD ** -0.5), (QK2 + 2, HD ** -0.5), (QK2 + 4, HD ** -0.5))):
                nc.vector.tensor_scalar(gq[:, i:i + 1], cols[:, src:src + 1], scale, None, ALU.mult).then_inc(set_dve, 1)
            nc.vector.memset(small[:, 6:7], 0.0).then_inc(set_dve, 1)
            for v, nh in enumerate((16, 4, 4, 4)):
                dve.wait_ge(tab_done, v + 1)
                nc.vector.tensor_copy(tabs[0:nh, v, :], bank[v][0:nh, 0:TABLE]).then_inc(tab_copied, 1)
            conf_dve(dve, conf0)
            fox_dve(dve, fox)
            short_dve(dve, short)
            conf_dve(dve, conf1)
            mixers_dve(dve, mixers)
            ffn_dve(dve, ffn)
            for i in range(4):
                dve.wait_ge(set_done, 16 + i)
                src = bank[2 + i][:, :].rearrange("p (a b d) -> p b a d", a=2, b=TB)
                dst = xnat[:, :, 2 * i * P:(2 * i + 2) * P].rearrange("p b (a d) -> p b a d", a=2)
                for tb in range(TB):
                    nc.vector.tensor_copy(dst[:, tb, :, :], src[:, tb, :, :]).then_inc(set_dve, 1)

        @block.scalar
        def _(act):
            act.wait_ge(set_pool, 1)
            hi_to(act, 1)
            conf_act(act, conf0)
            fox_act(act, fox)
            short_act(act, short)
            conf_act(act, conf1)
            mixers_act(act, mixers)
            ffn_act(act, ffn)
            ov = out[0].rearrange("(b p) d -> p b d", p=P)
            for i in range(4):
                act.wait_ge(set_dve, 5 + 2 * i + 2)
                act.dma_start(ov[:, :, 2 * i * P:(2 * i + 2) * P], xnat[:, :, 2 * i * P:(2 * i + 2) * P]).then_inc(out_stored, 16)
            act.wait_ge(out_stored, 64)


_INS = ["x", "a_norm", "a_w_in", "a_conv_w", "a_conv_b", "a_ln_g", "a_ln_b", "a_w_out", "b_norm", "b_w_in", "b_f_bias",
        "b_q_norm", "b_k_norm", "b_w_out", "c_norm", "c_w_in", "c_conv_w", "c_w_out", "norm1_g_2", "norm2_g_2",
        "w_in_2", "qk_norm_g_2", "nsa_cmp_pos_2", "nsa_cmp_w_2", "w_branch_a_2", "w_branch_b_2", "w_branch_c_2",
        "w_out_2", "w_ffn_in_2", "w_ffn_out_2", "rel_bias_2"]


def kernel(**inputs):
    import numpy as _np
    import concourse.bacc as _bacc
    from concourse import mybir as _mybir
    from concourse.bass_utils import run_bass_kernel_spmd as _run

    nc = _bacc.Bacc("TRN2", target_bir_lowering=False, num_devices=1)
    arrays, args = {}, {}
    cst, hot, sel = constants()
    given = [(name, _np.ascontiguousarray(inputs[name])) for name in _INS] + [("cst", cst), ("hot", hot), ("sel", sel)]
    for name, a in given:
        arrays[f"in_{name}_dram"] = a
        args[name] = nc.dram_tensor(f"in_{name}_dram", a.shape, _mybir.dt.from_np(a.dtype), kind="ExternalInput").ap()
    out = nc.dram_tensor("out_0_dram", (1, S, D), F32, kind="ExternalOutput").ap()
    program(nc, args, out)
    r = _run(nc, [arrays], core_ids=[0])
    return r.results[0]["out_0_dram"]
```
